# Optimizing a Trainium2 kernel written in Bass

```python
import math
import jax, jax.numpy as jnp
from jax import lax
import numpy as np

D_MODEL = 1024
BATCH = 1
SEQ = 1024
DEPTH = 1
DEC_BATCH = 8
DEC_SEQ = 8
PAST_LEN = 8192
PAGE_SIZE = 128

H_A = 4
DK_A = 128
DV_A = 128
W_A = H_A * DV_A
H_B = 8
HD_B = 64
W_B = H_B * HD_B
D_MIX = W_A + W_B
CONV_W = 4
MLSTM_CHUNK = 64
DIL_PATTERNS = ((128, 1), (512, 4), (2048, 16))
WIN_MAX = 2048
N_BUCKETS = 32
MAX_DIST = WIN_MAX
PEER_HEADS = 8
PEER_DQ = 256
N_SUBKEYS = 128
N_EXPERTS = N_SUBKEYS * N_SUBKEYS
PEER_TOPK = 16
PEER_BLOCK = 256
EPS = 1e-6
NEG = -1e30
SPLITS = (W_B, 2 * W_B, 3 * W_B, 3 * W_B + 2 * W_A, 3 * W_B + 3 * W_A, 3 * W_B + 4 * W_A, 3 * W_B + 4 * W_A + H_A)
W_IN = 3 * W_B + 4 * W_A + 2 * H_A

kernel_name = 'hymba_mlstm_dilated_peer_step'

def rmsnorm(x, g):
    xf = x.astype(jnp.float32)
    y = xf * lax.rsqrt(jnp.mean(xf * xf, axis=-1, keepdims=True) + EPS)
    return (y * g.astype(jnp.float32)).astype(x.dtype)

def t5_bucket(dist):
    max_exact = N_BUCKETS // 2
    d = np.maximum(dist, 1).astype(np.float32)
    large = max_exact + (np.log(d / max_exact) / math.log(MAX_DIST / max_exact) * (N_BUCKETS - max_exact)).astype(np.int32)
    large = np.minimum(large, N_BUCKETS - 1)
    return np.where(dist < max_exact, dist, large).astype(np.int32)

def last_rows(a, n):
    t = a.shape[1]
    if t >= n:
        return a[:, t - n:]
    return jnp.pad(a, ((0, 0), (n - t, 0)) + ((0, 0),) * (a.ndim - 2))

def dilated_branch_prompt(q, k, v, rel_bias, window, dil):
    B, T, H, hd = q.shape
    steps = window // dil
    n = T // dil
    nb = -(-n // steps)
    npad = nb * steps

    def to_band(a):
        a = a.reshape(B, n, dil, H, hd)
        a = jnp.pad(a, ((0, 0), (0, npad - n), (0, 0), (0, 0), (0, 0)))
        return a.reshape(B, nb, steps, dil, H, hd)

    def with_prev(a):
        prev = jnp.pad(a, ((0, 0), (1, 0), (0, 0), (0, 0), (0, 0), (0, 0)))[:, :nb]
        return jnp.concatenate([prev, a], axis=2)

    qb = to_band(q)
    kk = with_prev(to_band(k))
    vv = with_prev(to_band(v))
    qi = np.arange(steps)[:, None]
    kj = np.arange(2 * steps)[None, :]
    jstep = steps + qi - kj
    band = (jstep >= 0) & (jstep <= steps)
    mask = band[None] & ~((np.arange(nb)[:, None, None] == 0) & (kj[None] < steps))
    bias = jnp.moveaxis(rel_bias[t5_bucket(np.clip(jstep, 0, steps) * dil)].astype(jnp.float32), -1, 0)
    logits = jnp.einsum('bnqrhd,bnkrhd->bnrhqk', qb, kk) * (hd ** -0.5) + bias
    logits = jnp.where(mask[None, :, None, None], logits, NEG)
    mx = jnp.max(logits, axis=-1, keepdims=True)
    p = jnp.exp(logits - mx)
    den = jnp.sum(p, axis=-1)
    o = jnp.einsum('bnrhqk,bnkrhd->bnqrhd', p, vv) / jnp.moveaxis(den, -1, 2)[..., None]
    lse = jnp.moveaxis(mx[..., 0] + jnp.log(den), -1, 2)
    o = o.reshape(B, npad * dil, H, hd)[:, :T]
    lse = lse.reshape(B, npad * dil, H)[:, :T]
    return o, lse

def dilated_branch_sample(q, k_all, v_all, rel_bias, window, dil, buf_len):
    B, S, H, hd = q.shape
    steps = window // dil
    j = np.arange(steps + 1)
    idx = buf_len + np.arange(S)[:, None] - j[None, :] * dil
    valid = idx >= 0
    idx_c = np.maximum(idx, 0)
    kg = k_all[:, idx_c]
    vg = v_all[:, idx_c]
    bias = rel_bias[t5_bucket(j * dil)].astype(jnp.float32).T
    logits = jnp.einsum('bshd,bsjhd->bshj', q, kg) * (hd ** -0.5) + bias
    logits = jnp.where(valid[None, :, None, :], logits, NEG)
    mx = jnp.max(logits, axis=-1, keepdims=True)
    p = jnp.exp(logits - mx)
    den = jnp.sum(p, axis=-1)
    o = jnp.einsum('bshj,bsjhd->bshd', p, vg) / den[..., None]
    lse = mx[..., 0] + jnp.log(den)
    return o, lse

def combine_branches(branches):
    outs = jnp.stack([o for o, _ in branches], axis=0)
    lses = jnp.stack([l for _, l in branches], axis=0)
    wts = jax.nn.softmax(lses, axis=0)
    return jnp.einsum('pbth,pbthd->bthd', wts, outs)

def short_conv(u, buf, conv_w, conv_b):
    t = u.shape[1]
    ext = jnp.concatenate([buf.astype(u.dtype), u], axis=1)
    y = conv_b
    for j in range(CONV_W):
        y = y + ext[:, j:j + t] * conv_w[j]
    return jax.nn.silu(y), ext[:, ext.shape[1] - (CONV_W - 1):]

def mlstm(q, k, v, ig, lf, C0, n0, m0):
    B, T, H, _ = q.shape
    L = math.gcd(T, MLSTM_CHUNK)
    nc = T // L
    f32 = jnp.float32

    def chunks(a):
        a = a.astype(f32).reshape((B, nc, L, H) + a.shape[3:])
        return jnp.moveaxis(a, (1, 3), (0, 2))

    causal = jnp.asarray(np.tril(np.ones((L, L), dtype=bool)))

    def step(carry, xs):
        C, n, m = carry
        qc, kc, vc, igc, lfc = xs
        b = jnp.cumsum(lfc, axis=-1)
        g = b + m[..., None]
        D = jnp.where(causal, b[..., :, None] - b[..., None, :] + igc[..., None, :], -jnp.inf)
        mt = jnp.maximum(g, jnp.max(D, axis=-1))
        wD = jnp.exp(D - mt[..., None])
        wg = jnp.exp(g - mt)
        s = jnp.einsum('bhtd,bhsd->bhts', qc, kc) * wD
        num = wg[..., None] * jnp.einsum('bhtd,bhde->bhte', qc, C) + jnp.einsum('bhts,bhse->bhte', s, vc)
        den = wg * jnp.einsum('bhtd,bhd->bht', qc, n) + jnp.sum(s, axis=-1)
        h = num / jnp.maximum(jnp.abs(den), jnp.exp(-mt))[..., None]
        bL = b[..., -1]
        ws_log = bL[..., None] - b + igc
        m_new = jnp.maximum(bL + m, jnp.max(ws_log, axis=-1))
        ws = jnp.exp(ws_log - m_new[..., None])
        wc = jnp.exp(bL + m - m_new)
        C_new = wc[..., None, None] * C + jnp.einsum('bhsd,bhse->bhde', ws[..., None] * kc, vc)
        n_new = wc[..., None] * n + jnp.einsum('bhs,bhsd->bhd', ws, kc)
        return (C_new, n_new, m_new), h

    init = (C0.astype(f32), n0.astype(f32), m0.astype(f32))
    (C, n, m), hs = lax.scan(step, init, (chunks(q), chunks(k), chunks(v), chunks(ig), chunks(lf)))
    h = jnp.moveaxis(hs, (0, 2), (1, 3)).reshape(B, T, H, hs.shape[-1])
    return h, C, n, m

def peer(h, w_q, sub_keys, u_tab, v_tab):
    B, T, D = h.shape
    xt = h.reshape(B * T, D)
    ntok = xt.shape[0]
    npad = (-ntok) % PEER_BLOCK
    xb = jnp.pad(xt, ((0, npad), (0, 0))).reshape(-1, PEER_BLOCK, D)
    K = PEER_TOPK

    def block(xblk):
        qh = (xblk @ w_q).reshape(PEER_BLOCK, PEER_HEADS, 2, PEER_DQ // 2)
        s = jnp.einsum('nhpd,pkd->nhpk', qh, sub_keys).astype(jnp.float32)
        sv, si = lax.top_k(s, K)
        cand = (sv[:, :, 0, :, None] + sv[:, :, 1, None, :]).reshape(PEER_BLOCK, PEER_HEADS, K * K)
        cidx = (si[:, :, 0, :, None] * N_SUBKEYS + si[:, :, 1, None, :]).reshape(PEER_BLOCK, PEER_HEADS, K * K)
        fv, fpos = lax.top_k(cand, K)
        eidx = jnp.take_along_axis(cidx, fpos, axis=-1)
        gate = jax.nn.softmax(fv, axis=-1)
        act = jax.nn.gelu(jnp.einsum('nd,nhkd->nhk', xblk, u_tab[eidx]), approximate=False)
        return jnp.einsum('nhk,nhkd->nd', (gate * act).astype(xblk.dtype), v_tab[eidx])

    out = lax.map(block, xb).reshape(-1, D)[:ntok]
    return out.reshape(B, T, D)

def hybrid_layer(x, c, k_buf, v_buf, conv_buf, C0, n0, m0, rel_bias, w_ada, b_ada, norm1_g, norm2_g, w_in,
                 b_gate, conv_w, conv_b, q_norm_g, k_norm_g, att_out_g, mlstm_out_g, w_out, peer_wq,
                 peer_keys, peer_u, peer_v, buf_len):
    B, T, _ = x.shape
    f32 = jnp.float32
    mod = jax.nn.silu(c) @ w_ada + b_ada
    shift1, scale1, gate1, shift2, scale2, gate2 = jnp.split(mod[:, None, :], 6, axis=-1)
    h = rmsnorm(x, norm1_g) * (1 + scale1) + shift1
    aq, ak, av, mqk, mv, mo, mi, mf = jnp.split(h @ w_in, SPLITS, axis=-1)

    aq = rmsnorm(aq.reshape(B, T, H_B, HD_B).astype(f32), q_norm_g)
    ak = rmsnorm(ak.reshape(B, T, H_B, HD_B).astype(f32), k_norm_g)
    av = av.reshape(B, T, H_B, HD_B).astype(f32)
    if k_buf is None:
        att = combine_branches([dilated_branch_prompt(aq, ak, av, rel_bias, w, d) for w, d in DIL_PATTERNS])
        k_new = last_rows(ak, buf_len)
        v_new = last_rows(av, buf_len)
    else:
        k_all = jnp.concatenate([k_buf.astype(f32), ak], axis=1)
        v_all = jnp.concatenate([v_buf.astype(f32), av], axis=1)
        L0 = k_buf.shape[1]
        att = combine_branches([dilated_branch_sample(aq, k_all, v_all, rel_bias, w, d, L0) for w, d in DIL_PATTERNS])
        k_new = last_rows(k_all, buf_len)
        v_new = last_rows(v_all, buf_len)
    att = rmsnorm(att, att_out_g)

    if conv_buf is None:
        conv_buf = jnp.zeros((B, CONV_W - 1, 2 * W_A), x.dtype)
        C0 = jnp.zeros((B, H_A, DK_A, DV_A), f32)
        n0 = jnp.zeros((B, H_A, DK_A), f32)
        m0 = jnp.zeros((B, H_A), f32)
    qk, conv_new = short_conv(mqk, conv_buf, conv_w, conv_b)
    qk = qk.astype(f32).reshape(B, T, 2, H_A, DK_A)
    mq = qk[:, :, 0]
    mk = qk[:, :, 1] * (DK_A ** -0.5)
    mv = mv.reshape(B, T, H_A, DV_A)
    ig = mi.astype(f32) + b_gate[:H_A].astype(f32)
    lf = jax.nn.log_sigmoid(mf.astype(f32) + b_gate[H_A:].astype(f32))
    hA, C_new, n_new, m_new = mlstm(mq, mk, mv, ig, lf, C0, n0, m0)
    hA = rmsnorm(hA, mlstm_out_g) * jax.nn.sigmoid(mo.astype(f32)).reshape(B, T, H_A, DV_A)

    mix = jnp.concatenate([hA.reshape(B, T, W_A), att.reshape(B, T, W_B)], axis=-1).astype(x.dtype) @ w_out
    x = x + gate1 * mix
    h2 = rmsnorm(x, norm2_g) * (1 + scale2) + shift2
    x = x + gate2 * peer(h2, peer_wq, peer_keys, peer_u, peer_v)
    return x, (k_new, v_new, conv_new, C_new, n_new, m_new)

def setup_inputs(seed: int = 0) -> dict:
    key = jax.random.key(seed)
    ks = iter(jax.random.split(key, 40))

    def rnd(shape, scale):
        return jax.random.normal(next(ks), shape, jnp.float32) * scale

    wbuf = min(WIN_MAX, PAST_LEN)
    D = D_MODEL
    inputs = {
        'x_prompt': rnd((BATCH, SEQ, D), 1.0),
        'x_sample': rnd((DEC_BATCH, DEC_SEQ, D), 1.0),
        'cache_k': rnd((DEPTH, DEC_BATCH, wbuf, H_B, HD_B), 1.0),
        'cache_v': rnd((DEPTH, DEC_BATCH, wbuf, H_B, HD_B), 1.0),
        'state_conv': rnd((DEPTH, DEC_BATCH, CONV_W - 1, 2 * W_A), 1.0),
        'state_C': rnd((DEPTH, DEC_BATCH, H_A, DK_A, DV_A), 0.5),
        'state_n': rnd((DEPTH, DEC_BATCH, H_A, DK_A), 0.5),
        'state_m': rnd((DEPTH, DEC_BATCH, H_A), 1.0),
        'c_prompt': rnd((BATCH, D), 1.0),
        'c_sample': rnd((DEC_BATCH, D), 1.0),
        'rel_bias': rnd((N_BUCKETS, H_B), 0.5),
        'w_ada': rnd((DEPTH, D, 6 * D), 0.5 * D ** -0.5),
        'b_ada': rnd((DEPTH, 6 * D), 0.01),
        'norm1_g': 1.0 + rnd((DEPTH, D), 0.02),
        'norm2_g': 1.0 + rnd((DEPTH, D), 0.02),
        'w_in': rnd((DEPTH, D, W_IN), D ** -0.5),
        'b_gate': jnp.concatenate([rnd((DEPTH, H_A), 0.1),
                                   jnp.linspace(3.0, 6.0, H_A, dtype=jnp.float32) + rnd((DEPTH, H_A), 0.1)], axis=-1),
        'conv_w': rnd((DEPTH, CONV_W, 2 * W_A), CONV_W ** -0.5),
        'conv_b': rnd((DEPTH, 2 * W_A), 0.01),
        'q_norm_g': 1.0 + rnd((DEPTH, HD_B), 0.02),
        'k_norm_g': 1.0 + rnd((DEPTH, HD_B), 0.02),
        'att_out_g': 1.0 + rnd((DEPTH, H_B, HD_B), 0.02),
        'mlstm_out_g': 1.0 + rnd((DEPTH, H_A, DV_A), 0.02),
        'w_out': rnd((DEPTH, D_MIX, D), D_MIX ** -0.5),
        'peer_wq': rnd((DEPTH, D, PEER_HEADS * PEER_DQ), D ** -0.5),
        'peer_keys': rnd((DEPTH, 2, N_SUBKEYS, PEER_DQ // 2), (PEER_DQ // 2) ** -0.5),
        'peer_u': rnd((DEPTH, N_EXPERTS, D), D ** -0.5),
        'peer_v': rnd((DEPTH, N_EXPERTS, D), PEER_HEADS ** -0.5),
    }
    return inputs

def reference(x_prompt, x_sample, cache_k, cache_v, state_conv, state_C, state_n, state_m, c_prompt, c_sample,
              rel_bias, w_ada, b_ada, norm1_g, norm2_g, w_in, b_gate, conv_w, conv_b, q_norm_g, k_norm_g,
              att_out_g, mlstm_out_g, w_out, peer_wq, peer_keys, peer_u, peer_v):
    buf_len = cache_k.shape[2]
    yp = x_prompt
    ys = x_sample
    sp_list = []
    ss_list = []
    for l in range(DEPTH):
        yp, sp = hybrid_layer(yp, c_prompt, None, None, None, None, None, None, rel_bias,
                              w_ada[l], b_ada[l], norm1_g[l], norm2_g[l], w_in[l], b_gate[l], conv_w[l], conv_b[l],
                              q_norm_g[l], k_norm_g[l], att_out_g[l], mlstm_out_g[l], w_out[l], peer_wq[l],
                              peer_keys[l], peer_u[l], peer_v[l], buf_len)
        ys, ss = hybrid_layer(ys, c_sample, cache_k[l], cache_v[l], state_conv[l], state_C[l], state_n[l],
                              state_m[l], rel_bias,
                              w_ada[l], b_ada[l], norm1_g[l], norm2_g[l], w_in[l], b_gate[l], conv_w[l], conv_b[l],
                              q_norm_g[l], k_norm_g[l], att_out_g[l], mlstm_out_g[l], w_out[l], peer_wq[l],
                              peer_keys[l], peer_u[l], peer_v[l], buf_len)
        sp_list.append(sp)
        ss_list.append(ss)
    k_p, v_p, conv_p, C_p, n_p, m_p = [jnp.stack([s[i] for s in sp_list], axis=0) for i in range(6)]
    k_s, v_s, conv_s, C_s, n_s, m_s = [jnp.stack([s[i] for s in ss_list], axis=0) for i in range(6)]
    return (yp, ys, k_p, v_p, conv_p, C_p, n_p, m_p, k_s, v_s, conv_s, C_s, n_s, m_s)


_drawn_inputs = setup_inputs


def setup_inputs(seed=0):
    import zlib

    import numpy as np

    out = dict(_drawn_inputs(seed))
    spreads = {}
    factors = {'norm2_g': 7.383,
     'conv_b': 3.452,
     'q_norm_g': 8.0,
     'k_norm_g': 3.599,
     'att_out_g': 8.0,
     'mlstm_out_g': 8.0}
    for name, (base, spread) in spreads.items():
        noise = np.random.default_rng([zlib.crc32(name.encode()), seed]).standard_normal(out[name].shape)
        drawn = base * np.exp(spread * noise) if base else spread * noise
        out[name] = __import__('jax').numpy.asarray(drawn.astype(out[name].dtype))
    for name, factor in factors.items():
        out[name] = (out[name] * factor).astype(out[name].dtype)
    return out
```

```python
import math
from contextlib import ExitStack

import concourse.bass as bass
import numpy as np
from concourse import mybir

F32 = mybir.dt.float32
U32 = mybir.dt.uint32
ALU = mybir.AluOpType
ACT = mybir.ActivationFunctionType
AX = mybir.AxisListType

P = 128
D = 1024
KD = D // P
SEQ = 1024
NT = SEQ // P
DB, DS = 8, 8
NS = DB * DS
NTOK = SEQ + NS
H_A, DK = 4, 128
H_B, HD = 8, 64
W_A, W_B = H_A * DK, H_B * HD
W_IN = 3 * W_B + 4 * W_A + 2 * H_A
O_QK, O_MV, O_MO, O_G = 3 * W_B, 3 * W_B + 2 * W_A, 3 * W_B + 3 * W_A, 3 * W_B + 4 * W_A
CONV_W = 4
HALO = CONV_W - 1
WBUF = 2048
PAST = 2048
PATTERNS = ((128, 1), (512, 4), (2048, 16))
N_BUCKETS = 32
EPS = 1e-6
NEG = -1e30
NC9 = 1 + DB
OLD = WBUF - 512
ROWS_OLD = OLD // 16 * DS
ROWS = ROWS_OLD + 512
KT_ROWS = ROWS // P
DMAX = PAST + DS - 1
LTAB = DMAX + P
HEADS = 8
TOPK = 16
NKEY = 128
PICKS = HEADS * TOPK


def constants():
    s = np.arange(P)
    eye = np.eye(P)
    parts = {"ident": eye, "ones": np.ones((P, P))}
    seq = s // DS

    def kind(name, same, last):
        n = same.shape[0]
        causal = same & (s[:n, None] <= s[None, :n])
        full = np.zeros((4, P, n))
        full[0, :n] = causal
        full[1, :n] = np.where(causal, 0.0, NEG)
        full[2, :n] = np.where(causal.T, 0.0, NEG)
        full[3, :n] = last
        parts[name + "_tri"], parts[name + "_negT"], parts[name + "_neg"], parts[name + "_sel"] = full
        whole = np.zeros((P, n))
        whole[:n] = same
        parts[name + "_all"] = whole

    kind("p", np.ones((P, P), bool), np.repeat((s == P - 1)[:, None], P, 1))
    t = s[:NS]
    kind("s", seq[:NS, None] == seq[None, :NS], t[:, None] == DS * (t[None] // DS) + DS - 1)
    parts["member"] = (seq[:, None] == np.arange(DB)[None]) * (s < NS)[:, None]
    parts["headmask"] = ((s // DS)[:, None] == np.arange(H_B)[None]) * (s < NS)[:, None]
    parts["flip"] = eye[::-1]
    flip8 = np.zeros((P, NS))
    flip8[t, DS * (t // DS) + DS - 1 - t % DS] = 1.0
    parts["flip8"] = flip8
    parts["eps"] = np.full((P, 1), EPS)
    parts["lnscale"] = np.full((P, 1), math.log(DK ** -0.5))
    parts["iota16"] = np.repeat(np.arange(TOPK)[None], P, 0)
    place, at = {}, 0
    for name, a in parts.items():
        place[name] = (at, a.shape[1])
        at += a.shape[1]
    table = np.concatenate([np.asarray(a, np.float32) for a in parts.values()], 1)
    dist = DMAX - np.arange(LTAB)
    exact = N_BUCKETS // 2
    d = np.maximum(dist, 1).astype(np.float32)
    large = exact + (np.log(d / exact) / math.log(2048 / exact) * (N_BUCKETS - exact)).astype(np.int32)
    bucket = np.where(dist < exact, dist, np.minimum(large, N_BUCKETS - 1))
    count = sum(((dist >= 0) & (dist <= w) & (dist % r == 0)).astype(np.float64) for w, r in PATTERNS)
    onehot = np.zeros((P, LTAB), np.float32)
    onehot[:N_BUCKETS] = (bucket[None] == np.arange(N_BUCKETS)[:, None]) & (count > 0)[None]
    onehot[N_BUCKETS] = np.where(count > 0, np.log(np.maximum(count, 1)), NEG)
    return table, place, onehot


class Region:

    def __init__(self, mem, start, end):
        self.mem, self.at, self.end = mem, start, end

    def take(self, *shape):
        n = int(np.prod(shape))
        assert self.at + n <= self.end, (self.at, n, self.end)
        ap = self.mem[:, self.at:self.at + n]
        self.at += n
        if len(shape) == 1:
            return ap
        names = "abcd"[:len(shape)]
        left = " ".join(names)
        return ap.rearrange(f"p ({left}) -> p {left}", **dict(zip(names, shape)))


class Signals(dict):

    def __init__(self, nc):
        super().__init__()
        self.nc, self.stage = nc, 0

    def __missing__(self, name):
        self[name] = self.nc.alloc_semaphore(name=f"{name}.{self.stage}")
        return self[name]

    def retire(self, keep=()):
        names = [n for n in self if n not in keep]
        self.stage += 1
        self.nc.all_engine_barrier()
        self.nc.clear_and_free_semaphores([self.pop(n) for n in names])
        self.nc.all_engine_barrier()


def apart(eng, sem):
    eng.sem_inc(sem, 1)


class Chain:

    def __init__(self, eng, sem, done=0):
        self.eng, self.sem, self.done, self.n = eng, sem, done, 0

    def step(self, ins):
        ins.then_inc(self.sem, 1)
        self.n += 1

    def wait(self):
        self.eng.wait_ge(self.sem, self.done + self.n)

    def link(self, ins):
        self.step(ins)
        self.wait()


def bc(ap, axis, n):
    v = ap.unsqueeze(axis)
    shape = list(v.shape)
    shape[axis] = n
    return v.broadcast_to(tuple(shape))


CONST, PLACE, ONEHOT = constants()
N_CONST = CONST.shape[1]
MEM = 53120
END_SMALL = N_CONST + 1400
END_W = END_SMALL + KD * W_IN
ADA_CHUNK = 512
N_ADA = 6 * D // ADA_CHUNK
PER_P, PER_S = 59, 59
N_FLIPS = 2 * H_B + -(-ROWS // 512) + 1
PER_SEARCH, PER_TILE = 154, 155


def layer(nc, ins, outs):
    with ExitStack() as ctx:
        mem = ctx.enter_context(nc.sbuf_tensor("mem", [P, MEM], F32))
        psum = ctx.enter_context(nc.psum_tensor("psum", [P, 8, 512], F32))
        sig = Signals(nc)
        scratch = {
            "mod": nc.dram_tensor("mod_rows", [NC9, 6 * D], F32),
            "bias": nc.dram_tensor("bias_rows", [H_B, LTAB], F32),
            "qkv": nc.dram_tensor("qkv_rows", [NTOK, 3 * W_B], F32),
            "mix": nc.dram_tensor("mix_rows", [NTOK, D], F32),
            "x1": nc.dram_tensor("x1_rows", [NTOK, D], F32),
        }
        small = Region(mem, 0, END_SMALL)
        table = small.take(N_CONST)
        const = {k: table[:, a:a + n] for k, (a, n) in PLACE.items()}
        const["qk_gain"] = small.take(2 * HD)
        const["gate_bias"] = small.take(2 * H_A)
        const["mo_gain"] = small.take(W_A)
        const["att_gain"] = small.take(W_B)
        const["conv"] = small.take(CONV_W + 1, 8)
        with nc.Block() as block:
            stage0(nc, block, sig, mem, psum, const, table, ins, scratch)
        sig.retire()
        with nc.Block() as block:
            stage1(nc, block, sig, mem, psum, const, ins, outs, scratch)
        sig.retire(keep=("cache_out",))
        with nc.Block() as block:
            stage2(nc, block, sig, mem, psum, const, ins, outs, scratch)
        sig.retire()
        with nc.Block() as block:
            stage3(nc, block, sig, mem, psum, const, ins, outs, scratch)


def stage0(nc, block, sig, mem, psum, const, table, ins, scratch):
    work = Region(mem, END_W, MEM)
    cond = work.take(KD, NC9)
    w = work.take(2, KD, ADA_CHUNK)
    bias = work.take(2, ADA_CHUNK)
    gain = work.take(2, ADA_CHUNK)
    onehot = work.take(LTAB)
    rel = work.take(H_B)
    rows = mem[:, END_SMALL:END_SMALL + 6 * D]
    tab = mem[:, END_SMALL + 6 * D:END_SMALL + 6 * D + LTAB]
    pieces = [(a, min(512, LTAB - a)) for a in range(0, LTAB, 512)]
    scale_of = {n: g for g, part in ((0, 1), (1, 4)) for n in range(part * D // ADA_CHUNK, (part + 1) * D // ADA_CHUNK)}
    landed = [16 * sum(2 + (j in scale_of) for j in range(n % 2, n + 1, 2)) for n in range(N_ADA)]

    @block.sync
    def _(sp):
        sp.dma_start(cond, ins["cond"]).then_inc(sig["cond_in"], 16)
        sp.dma_start(table, ins["const"]).then_inc(sig["const_in"], 16)
        sp.dma_start(onehot, ins["onehot"]).then_inc(sig["onehot_in"], 16)
        sp.dma_start(rel, ins["rel"]).then_inc(sig["onehot_in"], 16)
        for n in range(N_ADA):
            if n >= 2:
                sp.wait_ge(sig["mod_row"], n - 1)
            cols = slice(n * ADA_CHUNK, (n + 1) * ADA_CHUNK)
            sp.dma_start(w[:, n % 2], ins["w_ada"][:, :, cols]).then_inc(sig[f"ada_in{n % 2}"], 16)
            sp.dma_start(bias[0:NC9, n % 2], ins["b_ada"][:, cols].broadcast_to((NC9, ADA_CHUNK))).then_inc(sig[f"ada_in{n % 2}"], 16)
            if n in scale_of:
                gcols = slice(n * ADA_CHUNK % D, n * ADA_CHUNK % D + ADA_CHUNK)
                g = ins["norm_gain"][scale_of[n]:scale_of[n] + 1, gcols]
                sp.dma_start(gain[0:NC9, n % 2], g.broadcast_to((NC9, ADA_CHUNK))).then_inc(sig[f"ada_in{n % 2}"], 16)
        sp.wait_ge(sig["mod_row"], N_ADA)
        sp.dma_start(scratch["mod"].ap(), rows[0:NC9]).then_inc(sig["tables_out"], 16)
        sp.wait_ge(sig["bias_tab"], len(pieces))
        sp.dma_start(scratch["bias"].ap(), tab[0:H_B]).then_inc(sig["tables_out"], 16)
        sp.wait_ge(sig["tables_out"], 32)

    @block.scalar
    def _(act):
        act.dma_start(const["qk_gain"], ins["qk_gain"].broadcast_to((P, 2 * HD))).then_inc(sig["small_in"], 16)
        act.dma_start(const["gate_bias"], ins["b_gate"].broadcast_to((P, 2 * H_A))).then_inc(sig["small_in"], 16)
        act.dma_start(const["mo_gain"], ins["mo_gain"].broadcast_to((P, W_A))).then_inc(sig["small_in"], 16)
        act.dma_start(const["att_gain"], ins["att_gain"].broadcast_to((P, W_B))).then_inc(sig["small_in"], 16)
        act.dma_start(const["conv"], ins["conv"]).then_inc(sig["small_in"], 16)
        act.wait_ge(sig["cond_in"], 16)
        nc.scalar.activation(cond, cond, ACT.Silu).then_inc(sig["cond"], 1)
        act.wait_ge(sig["small_in"], 80)

    @block.tensor
    def _(pe):
        pe.wait_ge(sig["onehot_in"], 32)
        for n, (a, m) in enumerate(pieces):
            if n >= 2:
                pe.wait_ge(sig["bias_tab"], n - 1)
            nc.tensor.matmul(psum[0:H_B, 4 + n % 2, 0:m], rel, onehot[:, a:a + m], start=True, stop=True).then_inc(sig["bias_ps"], 1)
        pe.wait_ge(sig["cond"], 1)
        for n in range(N_ADA):
            pe.wait_ge(sig[f"ada_in{n % 2}"], landed[n])
            if n >= 2:
                pe.wait_ge(sig["mod_row"], n - 1)
            for k in range(KD):
                mm = nc.tensor.matmul(psum[0:NC9, n % 2, :], cond[:, k, :], w[:, n % 2, k, :], start=k == 0, stop=k == KD - 1)
            mm.then_inc(sig["mod_ps"], 1)

    @block.vector
    def _(dve):
        for n, (a, m) in enumerate(pieces):
            dve.wait_ge(sig["bias_ps"], n + 1)
            nc.vector.tensor_copy(tab[0:H_B, a:a + m], psum[0:H_B, 4 + n % 2, 0:m]).then_inc(sig["bias_tab"], 1)
        gains = 0
        for n in range(N_ADA):
            out = rows[0:NC9, n * ADA_CHUNK:(n + 1) * ADA_CHUNK]
            dve.wait_ge(sig["mod_ps"], n + 1)
            dve.wait_ge(sig[f"ada_in{n % 2}"], landed[n])
            if n not in scale_of:
                nc.vector.tensor_tensor(out, psum[0:NC9, n % 2, :], bias[0:NC9, n % 2], ALU.add).then_inc(sig["mod_row"], 1)
                continue
            gains += 1
            nc.vector.tensor_tensor(out, psum[0:NC9, n % 2, :], bias[0:NC9, n % 2], ALU.add).then_inc(sig["mod_sum"], 1)
            dve.wait_ge(sig["mod_sum"], gains)
            nc.vector.scalar_tensor_tensor(out=out, in0=out, scalar=1.0, in1=gain[0:NC9, n % 2], op0=ALU.add, op1=ALU.mult).then_inc(sig["mod_row"], 1)


def stage1(nc, block, sig, mem, psum, const, ins, outs, scratch):
    w_in = mem[:, END_SMALL:END_W].rearrange("p (k n) -> p k n", k=KD)
    work = Region(mem, END_W, MEM)
    mod = work.take(2, D)
    x = work.take(D)
    h = work.take(D)
    h_t = work.take(KD, P)
    qkv = work.take(3 * W_B)
    squares = work.take(D)
    ext = work.take(8 * (P + HALO))
    ext_p = ext.rearrange("p (c t) -> p c t", c=8)
    ext_s = ext[:, 0:8 * DB * (DS + HALO)].rearrange("p (c b t) -> p c b t", c=8, b=DB)
    conv = work.take(8, P)
    vaug = work.take(H_A, DK + 1)
    og = work.take(W_A)
    state = work.take(H_A, DK + 1)
    kws = diag_a = work.take(H_A, P)
    diag_m = work.take(H_A, P)
    diag_d = work.take(H_A, P)
    arg = work.take(H_A, P)
    decay_t = work.take(H_A, P)
    scores_t = work.take(H_A, P)
    carry = work.take(H_A, P)
    q_carry = work.take(H_A, P)
    hid = work.take(H_A, DK)
    gates = work.take(2 * H_A)
    sm = {n: work.take(H_A) for n in ("nabs", "soft", "lf", "b", "blast", "a", "a_s", "cmax", "m", "dm", "mlast", "wsarg", "ws",
                                      "wcarg", "mprev", "mnew", "den", "dneg", "bm", "floor", "dmax", "rden", "hss", "hln", "hrs")}
    xss, xln, xrs = work.take(1), work.take(1), work.take(1)
    qss, qln, qrs = work.take(16), work.take(16), work.take(16)
    conv_y = work.take(8, P)
    s_state = work.take(DB, H_A, DK + 1)
    num_t = diag_m[:, :, 0:NS]
    qn = diag_d[:, :, 0:NS]
    kws_of = h.rearrange("p (s h e) -> p s h e", s=2, h=H_A)

    def heads_ps(bank, rows, n=P):
        return psum[0:rows, bank, 0:H_A * n].rearrange("p (h t) -> p h t", h=H_A)

    def heads_of(buf, rows):
        return buf.rearrange("p h t -> p (h t)")[0:rows, 0:H_A * rows].rearrange("p (h t) -> p h t", h=H_A)

    def diag_a_of(rows):
        return diag_a.rearrange("p h t -> p (h t)")[0:rows, 0:H_A * rows]

    def diag_m_of(rows):
        return diag_m.rearrange("p h t -> p (h t)")[0:rows, 0:H_A * rows]

    def diag_d_of(rows):
        return diag_d.rearrange("p h t -> p (h t)")[0:rows, 0:H_A * rows]

    def arg_of(rows):
        return arg[0:rows, :, 0:rows]

    def s_update(dve, v, chain, b):
        dve.wait_ge(sig["s_cup"], b + 1)
        old = s_state[:, b]
        chain.link(v.tensor_tensor(old, old, bc(carry[:, :, b * DS + DS - 1], 2, DK + 1), ALU.mult))
        banks = ((2, 3), (4, 5))[b % 2]
        chain.step(v.tensor_tensor(old[:, 0:2], old[:, 0:2], num_ps(P, 0, banks), ALU.add))
        v.tensor_tensor(old[:, 2:4], old[:, 2:4], num_ps(P, 1, banks), ALU.add).then_inc(sig["s_state"], 1)

    def num_ps(rows, pair, banks):
        return psum[0:rows, banks[pair], 0:2 * (DK + 1)].rearrange("p (h e) -> p h e", h=2)

    @block.sync
    def _(sp):
        def tile(i, rows, first):
            sp.wait_ge(sig["h"], i)
            sp.dma_start(x[0:rows], first).then_inc(sig["x_in"], 16)

        row0 = scratch["mod"].ap()[0:1]
        sp.dma_start(mod[:, 0], row0[:, 0:D].broadcast_to((P, D))).then_inc(sig["mod_in"], 16)
        sp.dma_start(mod[:, 1], row0[:, D:2 * D].broadcast_to((P, D))).then_inc(sig["mod_in"], 16)
        tile(0, P, ins["x"][0:P, :])
        with sp.Fori(1, NT) as i:
            tile(i, P, ins["x"][bass.ds(i * P, P), :])
        sp.wait_ge(sig["h"], NT)
        per_seq = scratch["mod"].ap()[1:NC9]
        for part in range(2):
            src = bc(per_seq[:, part * D:(part + 1) * D], 1, DS)
            sp.dma_start(mod[0:NS, part], src).then_inc(sig["mod_in"], 16)
        tile(NT, NS, ins["x"][SEQ:NTOK, :])
        sp.wait_ge(sig["state"], NT)
        sp.dma_start(outs["state_p"], state).then_inc(sig["out1"], 16)
        sp.dma_start(outs["m_p"], sm["mprev"][0:1]).then_inc(sig["out1"], 16)
        sp.wait_ge(sig["halo"], NT)
        sp.dma_start(outs["conv_p"], ext_p[:, :, P:P + HALO]).then_inc(sig["conv_out"], 16)
        sp.dma_start(s_state, ins["state"]).then_inc(sig["s_state_in"], 16)
        sp.wait_ge(sig["out1"], 32)
        sp.dma_start(sm["mprev"][0:NS], ins["m0"]).then_inc(sig["s_state_in"], 16)
        sp.wait_ge(sig["conv_out"], 16)
        for c in range(8):
            sp.dma_start(ext_s[:, c, :, 0:HALO], ins["conv_tail"][:, c]).then_inc(sig["s_conv_in"], 16)
        sp.wait_ge(sig["s_ext"], 8)
        for c in range(8):
            sp.dma_start(outs["conv_s"][:, c], ext_s[:, c, :, DS:DS + HALO]).then_inc(sig["out1"], 16)
        sp.wait_ge(sig["mnew"], NT + 1)
        sp.dma_start(outs["m_s"], sm["mnew"][0:NS]).then_inc(sig["out1"], 16)
        sp.wait_ge(sig["s_state"], DB)
        sp.dma_start(outs["state_s"], s_state).then_inc(sig["out1"], 16)
        sp.wait_ge(sig["out1"], 16 * (2 + 8 + 2))

    @block.gpsimd
    def _(pool):
        def store(i, rows, at):
            pool.wait_ge(sig["qk_n"], i + 1)
            pool.wait_ge(sig["av"], i + 1)
            pool.dma_start(scratch["qkv"].ap()[at, :], qkv[0:rows]).then_inc(sig["qkv_out"], 16)
            pool.wait_ge(sig["hid"], i + 1)
            pool.dma_start(scratch["mix"].ap()[at, 0:W_A], hid[0:rows].rearrange("p h e -> p (h e)")).then_inc(sig["hid_out"], 16)

        store(0, P, slice(0, P))
        with pool.Fori(1, NT) as i:
            store(i, P, bass.ds(i * P, P))
        store(NT, NS, slice(SEQ, NTOK))
        pool.wait_ge(sig["qkv_out"], 16 * (NT + 1))
        pool.wait_ge(sig["hid_out"], 16 * (NT + 1))

    @block.scalar
    def _(act):
        for k in range(KD):
            act.dma_start(w_in[:, k], ins["w_in"][:, k]).then_inc(sig["w_in_in"], 16)
        for b in range(DB):
            for name in ("k_s", "v_s"):
                act.dma_start(outs[name][b, 0:WBUF - DS], ins["cache_" + name[0]][b, DS:WBUF]).then_inc(sig["cache_out"], 16)
        lnscale, eps = const["lnscale"], const["eps"]

        def tile(i, rows, kind, per):
            chain = Chain(act, sig["act1"], i * per)

            def inv_rms(out, tmp, total, n, event):
                chain.link(nc.scalar.activation(tmp, total, ACT.Ln, scale=1.0 / n, bias=eps[0:rows]))
                nc.scalar.activation(out, tmp, ACT.Exp, scale=-0.5).then_inc(sig[event], 1)

            act.wait_ge(sig["x_in"], (i + 1) * 16)
            act.wait_ge(sig["h"], i)
            chain.link(nc.scalar.activation(squares[0:rows], x[0:rows], ACT.Square, accum_out=xss[0:rows]))
            inv_rms(xrs[0:rows], xln[0:rows], xss[0:rows], D, "x_rms")
            act.wait_ge(sig["h_t_ps"], i + 1)
            act.wait_ge(sig["av_ps"], i)
            for half in range(2):
                src = psum[:, half].rearrange("p (k t) -> p k t", k=4)[:, :, 0:rows]
                cp = nc.scalar.activation(h_t[:, 4 * half:4 * half + 4, 0:rows], src, ACT.Copy)
                cp.then_inc(sig["h_t"], 1)
            act.wait_ge(sig["gates"], i + 1)
            chain.link(nc.scalar.activation(sm["nabs"][0:rows], gates[0:rows, H_A:], ACT.Abs))
            chain.link(nc.scalar.activation(sm["soft"][0:rows], sm["nabs"][0:rows], ACT.Exp, scale=-1.0))
            nc.scalar.activation(sm["soft"][0:rows], sm["soft"][0:rows], ACT.Ln, bias=1.0).then_inc(sig["soft"], 1)
            act.wait_ge(sig["mv_ps"], i + 1)
            act.wait_ge(sig["cup"], i)
            nc.scalar.activation(vaug[0:rows, :, 0:DK], heads_ps(5, rows, DK), ACT.Copy).then_inc(sig["vaug"], 1)
            act.wait_ge(sig["mo_ps"], i + 1)
            act.wait_ge(sig["hid"], i)
            nc.scalar.activation(og[0:rows], psum[0:rows, 6], ACT.Exp, scale=-1.0).then_inc(sig["og"], 1)
            act.wait_ge(sig["conv"], i + 1)
            act.wait_ge(sig["ktok_ps"], i)
            act.wait_ge(sig["qcarry"], i)
            nc.scalar.activation(conv[:, :, 0:rows], conv_y[:, :, 0:rows], ACT.Silu).then_inc(sig["silu"], 1)
            act.wait_ge(sig["arg"], i + 1)
            act.wait_ge(sig["scores"], i)
            for hh in range(H_A):
                e = nc.scalar.activation(decay_t[0:rows, hh, 0:rows], arg[0:rows, hh, 0:rows], ACT.Exp, bias=sm["a_s"][0:rows, hh:hh + 1])
            e.then_inc(sig["decay"], 1)
            act.wait_ge(sig["state"], i)
            nc.scalar.activation(carry[:, :, 0:rows], heads_ps(4, P, rows), ACT.Exp).then_inc(sig["carry"], 1)
            nc.scalar.activation(sm["ws"][0:rows], sm["wsarg"][0:rows], ACT.Exp).then_inc(sig["ws"], 1)
            nc.scalar.activation(sm["floor"][0:rows], sm["bm"][0:rows], ACT.Exp, scale=-1.0).then_inc(sig["floor"], 1)
            act.wait_ge(sig["qk_ps"], i + 1)
            act.wait_ge(sig["qss"], i)
            sq = squares[0:rows].rearrange("p (a n) -> p a n", a=2)
            nc.scalar.activation(sq, psum[0:rows, 2:4], ACT.Square).then_inc(sig["qsq"], 1)
            act.wait_ge(sig["qss"], i + 1)
            chain.link(nc.scalar.activation(qln[0:rows], qss[0:rows], ACT.Ln, scale=1.0 / HD, bias=eps[0:rows]))
            nc.scalar.activation(qrs[0:rows], qln[0:rows], ACT.Exp, scale=-0.5).then_inc(sig["qrs"], 1)
            act.wait_ge(sig["av_ps"], i + 1)
            act.wait_ge(sig["qkv_out"], i * 16)
            nc.scalar.activation(qkv[0:rows, 2 * W_B:], psum[0:rows, 4], ACT.Copy).then_inc(sig["av"], 1)
            if kind == "s":
                act.wait_ge(sig["num_t_ps"], 1)
                nc.scalar.activation(num_t, heads_ps(4, P, NS), ACT.Copy).then_inc(sig["num_t"], 1)
            act.wait_ge(sig["hraw"], i + 1)
            for hh in range(H_A):
                e = nc.scalar.activation(squares[0:rows, hh * DK:(hh + 1) * DK], hid[0:rows, hh], ACT.Square, accum_out=sm["hss"][0:rows, hh:hh + 1])
            chain.link(e)
            inv_rms(sm["hrs"][0:rows], sm["hln"][0:rows], sm["hss"][0:rows], DK, "h_rms")
            assert chain.n == per, chain.n

        tile(0, P, "p", 7)
        with act.Fori(1, NT) as i:
            tile(i, P, "p", 7)
        tile(NT, NS, "s", 7)

    @block.tensor
    def _(pe):
        ident, ones = const["ident"], const["ones"]

        def project(bank, col, n, rows, at=0):
            for k in range(KD):
                mm = nc.tensor.matmul(psum[0:rows, bank, at:at + n], h_t[:, k, 0:rows], w_in[:, k, col:col + n], start=k == 0, stop=k == KD - 1)
            return mm

        def tile(i, rows, kind):
            pe.wait_ge(sig["h"], i + 1)
            pe.wait_ge(sig["hraw"], i)
            pe.wait_ge(sig["kws"], i)
            for k in range(KD):
                tr = nc.tensor.transpose(psum[:, k // 4, k % 4 * P:k % 4 * P + rows], h[0:rows, k * P:(k + 1) * P], ident[0:rows, 0:rows])
            tr.then_inc(sig["h_t_ps"], 1)
            pe.wait_ge(sig["h_t"], 2 * i + 2)
            pe.wait_ge(sig["w_in_in"], 16 * KD)
            pe.wait_ge(sig["mnew"], i)
            project(7, O_G, 2 * H_A, rows).then_inc(sig["gates_ps"], 1)
            for c in range(8):
                for k in range(KD):
                    mm = nc.tensor.matmul(psum[:, c // 4, c % 4 * P:c % 4 * P + rows], w_in[:, k, O_QK + c * P:O_QK + (c + 1) * P],
                                          h_t[:, k, 0:rows], start=k == 0, stop=k == KD - 1)
            mm.then_inc(sig["mqk_ps"], 1)
            pe.wait_ge(sig["scores"], i)
            project(5, O_MV, W_A, rows).then_inc(sig["mv_ps"], 1)
            pe.wait_ge(sig["lf"], i + 1)
            nc.tensor.matmul(psum[0:rows, 7, 8:12], const[kind + "_tri"][0:rows, 0:rows], sm["lf"][0:rows], start=True, stop=True)
            nc.tensor.matmul(psum[0:rows, 7, 12:16], const[kind + "_all"][0:rows, 0:rows], sm["lf"][0:rows], start=True, stop=True).then_inc(sig["b_ps"], 1)
            project(6, O_MO, W_A, rows).then_inc(sig["mo_ps"], 1)
            pe.wait_ge(sig["diag_a"], i + 1)
            pe.wait_ge(sig["state"], i)
            nc.tensor.matmul(psum[0:rows, 2, 0:H_A * rows], ones[0:rows, 0:rows], diag_a_of(rows), start=True, stop=True).then_inc(sig["a_rep"], 1)
            pe.wait_ge(sig["diag_m"], i + 1)
            pe.wait_ge(sig["av"], i)
            nc.tensor.matmul(psum[0:rows, 3, 0:H_A * rows], ones[0:rows, 0:rows], diag_m_of(rows), start=True, stop=True)
            nc.tensor.matmul(psum[:, 4, 0:H_A * rows], ones[0:rows, :], diag_d_of(rows), start=True, stop=True)
            nc.tensor.matmul(psum[0:rows, 7, 16:20], const[kind + "_sel"][0:rows, 0:rows], sm["cmax"][0:rows], start=True, stop=True).then_inc(sig["m_rep"], 1)
            project(2, 0, W_B, rows)
            pe.wait_ge(sig["arg"], i + 1)
            project(3, W_B, W_B, rows).then_inc(sig["qk_ps"], 1)
            pe.wait_ge(sig["silu"], i + 1)
            pe.wait_ge(sig["vaug"], i + 1)
            for hh in range(H_A):
                mm = nc.tensor.matmul(psum[0:rows, 5, hh * rows:(hh + 1) * rows], conv[:, H_A + hh, 0:rows], conv[:, hh, 0:rows], start=True, stop=True)
            mm.then_inc(sig["s_ps"], 1)
            for hh in range(H_A):
                tr = nc.tensor.transpose(psum[0:rows, 1, hh * DK:(hh + 1) * DK], conv[:, H_A + hh, 0:rows], ident)
            tr.then_inc(sig["ktok_ps"], 1)
            pe.wait_ge(sig["carry"], i + 1)
            project(4, 2 * W_B, W_B, rows).then_inc(sig["av_ps"], 1)
            if kind == "s":
                pe.wait_ge(sig["av"], i + 1)
            pe.wait_ge(sig["scores"], i + 1)
            pe.wait_ge(sig["qcarry"], i + 1)
            pe.wait_ge(sig["og"], i + 1)
            if kind == "p":
                for hh in range(H_A):
                    out = num_ps(rows, hh // 2, (6, 0))[:, hh % 2]
                    nc.tensor.matmul(out, scores_t[0:rows, hh, 0:rows], vaug[0:rows, hh], start=True, stop=False)
                    mm = nc.tensor.matmul(out, q_carry[:, hh, 0:rows], state[:, hh], start=False, stop=True)
                mm.then_inc(sig["num_ps"], 1)
                pe.wait_ge(sig["kws"], i + 1)
                pe.wait_ge(sig["qk_n"], i + 1)
                for hh in range(H_A):
                    mm = nc.tensor.matmul(num_ps(P, hh // 2, (2, 3))[:, hh % 2], kws[0:rows, hh], vaug[0:rows, hh], start=True, stop=True)
                mm.then_inc(sig["cup"], 1)

        tile(0, P, "p")
        with pe.Fori(1, NT) as i:
            tile(i, P, "p")
        tile(NT, NS, "s")
        pe.wait_ge(sig["s_state_in"], 32)
        for hh in range(H_A):
            for b in range(DB):
                mm = nc.tensor.matmul(psum[:, 4, hh * NS + b * DS:hh * NS + (b + 1) * DS], s_state[:, b, hh, 0:DK],
                                      q_carry[:, hh, b * DS:(b + 1) * DS], start=True, stop=True)
        mm.then_inc(sig["num_t_ps"], 1)
        pe.wait_ge(sig["num_t"], 1)
        for hh in range(H_A):
            out = num_ps(NS, hh // 2, (6, 0))[:, hh % 2]
            nc.tensor.matmul(out, scores_t[0:NS, hh, 0:NS], vaug[0:NS, hh], start=True, stop=False)
            nc.tensor.matmul(out[:, 0:DK], num_t[:, hh], ident, start=False, stop=False)
            mm = nc.tensor.matmul(out[:, DK:DK + 1], qn[:, hh], ones[:, 0:1], start=False, stop=True)
        mm.then_inc(sig["num_ps"], 1)
        for b in range(DB):
            pe.wait_ge(sig["s_kws"], b + 1)
            if b >= 2:
                pe.wait_ge(sig["s_state"], b - 1)
            for hh in range(H_A):
                mm = nc.tensor.matmul(num_ps(P, hh // 2, ((2, 3), (4, 5))[b % 2])[:, hh % 2], kws_of[0:NS, b % 2, hh], vaug[0:NS, hh],
                                      start=True, stop=True)
            mm.then_inc(sig["s_cup"], 1)

    @block.vector
    def _(dve):
        v = nc.vector
        ident, lnscale = const["ident"], const["lnscale"]
        taps = const["conv"]

        def tile(i, rows, kind, per):
            chain = Chain(dve, sig["dve1"], dve_base + i * per)
            R = slice(0, rows)

            def s(name):
                return sm[name][R]

            dve.wait_ge(sig["x_rms"], i + 1)
            dve.wait_ge(sig["h_t_ps"], i)
            chain.link(v.scalar_tensor_tensor(out=h[R], in0=x[R], scalar=xrs[R], in1=mod[R, 1], op0=ALU.mult, op1=ALU.mult))
            v.tensor_tensor(h[R], h[R], mod[R, 0], ALU.add).then_inc(sig["h"], 1)
            dve.wait_ge(sig["gates_ps"], i + 1)
            v.tensor_tensor(gates[R], psum[R, 7, 0:2 * H_A], const["gate_bias"][R], ALU.add).then_inc(sig["gates"], 1)
            dve.wait_ge(sig["soft"], i + 1)
            v.scalar_tensor_tensor(out=s("lf"), in0=gates[R, H_A:], scalar=0.0, in1=s("soft"), op0=ALU.min, op1=ALU.subtract).then_inc(sig["lf"], 1)
            dve.wait_ge(sig["mqk_ps"], i + 1)
            dve.wait_ge(sig["silu"], i)
            if kind == "p":
                chain.link(v.tensor_copy(ext_p[:, :, HALO:], psum[:, 0:2].rearrange("p a (c t) -> p (a c) t", c=4)))
            else:
                for c in range(8):
                    v.tensor_copy(ext_s[:, c, :, HALO:], psum[:, c // 4, c % 4 * P:c % 4 * P + NS].rearrange("p (b t) -> p b t", b=DB)).then_inc(sig["s_ext"], 1)
                dve.wait_ge(sig["s_ext"], 8)
            for j in range(CONV_W):
                for c in range(8):
                    src = ext_p[:, c, j:j + P] if kind == "p" else ext_s[:, c, :, j:j + DS]
                    out = conv_y[:, c] if kind == "p" else conv_y[:, c, 0:NS].rearrange("p (b t) -> p b t", b=DB)
                    if j == 0:
                        op = v.tensor_scalar(out, src, taps[:, 0, c:c + 1], taps[:, CONV_W, c:c + 1], ALU.mult, ALU.add)
                    else:
                        op = v.scalar_tensor_tensor(out=out, in0=src, scalar=taps[:, j, c:c + 1], in1=out, op0=ALU.mult, op1=ALU.add)
                    if j < CONV_W - 1 or c < 7:
                        chain.step(op)
                if j < CONV_W - 1:
                    chain.wait()
            op.then_inc(sig["conv"], 1)
            dve.wait_ge(sig["conv"], i + 1)
            if kind == "p":
                v.tensor_copy(ext_p[:, :, 0:HALO], ext_p[:, :, P:P + HALO]).then_inc(sig["halo"], 1)
            dve.wait_ge(sig["b_ps"], i + 1)
            chain.step(v.tensor_copy(s("b"), psum[R, 7, 8:12]))
            chain.step(v.tensor_copy(s("blast"), psum[R, 7, 12:16]))
            chain.link(v.tensor_tensor(s("a"), gates[R, 0:H_A], psum[R, 7, 8:12], ALU.subtract))
            chain.step(v.tensor_scalar(s("a_s"), s("a"), lnscale[R], None, ALU.add))
            v.tensor_tensor(heads_of(diag_a, rows), bc(ident[R, R], 1, H_A), bc(s("a"), 2, rows), ALU.mult).then_inc(sig["diag_a"], 1)
            dve.wait_ge(sig["a_rep"], i + 1)
            if kind == "s":
                dve.wait_ge(sig["s_state_in"], 32)
            chain.link(v.tensor_tensor(arg_of(rows), heads_ps(2, rows, rows), bc(const[kind + "_neg"][R], 1, H_A), ALU.add))
            chain.link(v.tensor_reduce(s("cmax"), arg_of(rows), AX.X, ALU.max))
            chain.link(v.tensor_tensor(s("cmax"), s("cmax"), s("mprev"), ALU.max))
            chain.link(v.tensor_tensor(s("dm"), s("mprev"), s("cmax"), ALU.subtract))
            chain.step(v.tensor_tensor(s("bm"), s("b"), s("cmax"), ALU.add))
            chain.step(v.tensor_tensor(heads_of(diag_m, rows), bc(ident[R, R], 1, H_A), bc(s("cmax"), 2, rows), ALU.mult))
            chain.wait()
            v.tensor_tensor(heads_of(diag_d, rows), bc(ident[R, R], 1, H_A), bc(s("dm"), 2, rows), ALU.mult).then_inc(sig["diag_m"], 1)
            dve.wait_ge(sig["m_rep"], i + 1)
            chain.link(v.tensor_copy(s("mlast"), psum[R, 7, 16:20]))
            chain.step(v.tensor_tensor(s("wsarg"), s("a_s"), s("mlast"), ALU.subtract))
            v.tensor_tensor(s("mnew"), s("blast"), s("mlast"), ALU.add).then_inc(sig["mnew"], 1)
            chain.wait()
            v.tensor_tensor(arg_of(rows), bc(const[kind + "_negT"][R], 1, H_A), heads_ps(3, rows, rows), ALU.subtract).then_inc(sig["arg"], 1)
            dve.wait_ge(sig["og"], i + 1)
            chain.link(v.tensor_scalar(og[R], og[R], 1.0, None, ALU.add))
            chain.link(v.reciprocal(og[R], og[R]))
            chain.step(v.tensor_tensor(og[R], og[R], const["mo_gain"][R], ALU.mult))
            dve.wait_ge(sig["decay"], i + 1)
            dve.wait_ge(sig["s_ps"], i + 1)
            v.tensor_tensor(scores_t[R, :, R], heads_ps(5, rows, rows), decay_t[R, :, R], ALU.mult).then_inc(sig["scores"], 1)
            dve.wait_ge(sig["carry"], i + 1)
            op = v.tensor_tensor(q_carry[:, :, R], conv[:, 0:H_A, R], carry[:, :, R], ALU.mult)
            if kind == "s":
                chain.link(op)
                for hh in range(H_A):
                    op = v.tensor_tensor(qn[:, hh].rearrange("p (b t) -> p b t", b=DB), q_carry[:, hh, R].rearrange("p (b t) -> p b t", b=DB),
                                         bc(s_state[:, :, hh, DK], 2, DS), ALU.mult)
                    if hh < H_A - 1:
                        chain.step(op)
            op.then_inc(sig["qcarry"], 1)
            dve.wait_ge(sig["ktok_ps"], i + 1)
            dve.wait_ge(sig["ws"], i + 1)
            v.tensor_tensor(kws[R], heads_ps(1, rows, DK), bc(s("ws"), 2, DK), ALU.mult).then_inc(sig["kws"], 1)
            dve.wait_ge(sig["qsq"], i + 1)
            v.tensor_reduce(qss[R], squares[R].rearrange("p (g e) -> p g e", e=HD), AX.X, ALU.add).then_inc(sig["qss"], 1)
            dve.wait_ge(sig["qrs"], i + 1)
            dve.wait_ge(sig["qkv_out"], i * 16)
            qk = qkv[R, 0:2 * W_B].rearrange("p (g e) -> p g e", e=HD)
            chain.link(v.tensor_tensor(qk, psum[R, 2:4].rearrange("p a (g e) -> p (a g) e", e=HD), bc(qrs[R], 2, HD), ALU.mult))
            gain = bc(const["qk_gain"][R].rearrange("p (a e) -> p a e", a=2), 2, H_B)
            qk4 = qkv[R, 0:2 * W_B].rearrange("p (a g e) -> p a g e", a=2, e=HD)
            v.tensor_tensor(qk4, qk4, gain, ALU.mult).then_inc(sig["qk_n"], 1)
            dve.wait_ge(sig["num_ps"], i + 1)
            dve.wait_ge(sig["floor"], i + 1)
            dve.wait_ge(sig["hid_out"], i * 16)
            for pair in range(2):
                chain.step(v.tensor_copy(s("den")[:, 2 * pair:2 * pair + 2], num_ps(rows, pair, (6, 0))[:, :, DK]))
            chain.wait()
            chain.link(v.scalar_tensor_tensor(out=s("dmax"), in0=s("den"), scalar=-1.0, in1=s("den"), op0=ALU.mult, op1=ALU.max))
            chain.link(v.tensor_tensor(s("dmax"), s("dmax"), s("floor"), ALU.max))
            chain.link(v.reciprocal(s("rden"), s("dmax")))
            for pair in range(2):
                op = v.tensor_tensor(hid[R, 2 * pair:2 * pair + 2], num_ps(rows, pair, (6, 0))[:, :, 0:DK], bc(s("rden")[:, 2 * pair:2 * pair + 2], 2, DK), ALU.mult)
                if pair == 0:
                    chain.step(op)
            op.then_inc(sig["hraw"], 1)
            dve.wait_ge(sig["h_rms"], i + 1)
            chain.link(v.tensor_tensor(hid[R], hid[R], bc(s("hrs"), 2, DK), ALU.mult))
            v.tensor_tensor(hid[R], hid[R], og[R].rearrange("p (h e) -> p h e", h=H_A), ALU.mult).then_inc(sig["hid"], 1)
            if kind == "p":
                dve.wait_ge(sig["cup"], i + 1)
                chain.link(v.tensor_tensor(state, state, bc(carry[:, :, P - 1], 2, DK + 1), ALU.mult))
                chain.step(v.tensor_tensor(state[:, 0:2], state[:, 0:2], num_ps(P, 0, (2, 3)), ALU.add))
                chain.step(v.tensor_copy(s("mprev"), s("mnew")))
                chain.wait()
                v.tensor_tensor(state[:, 2:4], state[:, 2:4], num_ps(P, 1, (2, 3)), ALU.add).then_inc(sig["state"], 1)
            assert chain.n == per, (kind, chain.n)

        v.memset(state, 0.0).then_inc(sig["dve1"], 1)
        v.memset(ext_p[:, :, 0:HALO], 0.0).then_inc(sig["dve1"], 1)
        v.memset(vaug[:, :, DK], 1.0).then_inc(sig["dve1"], 1)
        v.memset(sm["mprev"], 0.0).then_inc(sig["dve1"], 1)
        dve_base = 4
        dve.wait_ge(sig["dve1"], dve_base)
        dve.wait_ge(sig["mod_in"], 32)
        tile(0, P, "p", PER_P)
        with dve.Fori(1, NT) as i:
            tile(i, P, "p", PER_P)
        dve.wait_ge(sig["mod_in"], 64)
        dve.wait_ge(sig["s_conv_in"], 16 * 8)
        dve_base += NT * (PER_P - PER_S)
        tile(NT, NS, "s", PER_S)
        chain = Chain(dve, sig["s_state_steps"])
        for b in range(DB):
            if b >= 2:
                dve.wait_ge(sig["s_cup"], b - 1)
            v.tensor_scalar(kws_of[0:NS, b % 2], kws[0:NS], const["member"][0:NS, b:b + 1], None, ALU.mult).then_inc(sig["s_kws"], 1)
            if b >= 1:
                s_update(dve, v, chain, b - 1)
        s_update(dve, v, chain, DB - 1)


def stage2(nc, block, sig, mem, psum, const, ins, outs, scratch):
    front = Region(mem, END_SMALL, END_W)
    rest = Region(mem, END_W, MEM)
    qkv = rest.take(NT, 3 * W_B)
    q_t = rest.take(4, SEQ)
    k_t = rest.take(4, SEQ)
    bias = front.take(H_B, SEQ)
    probs = front.take(2, SEQ)
    probs_t = front.take(2, NT, P)
    kv0 = front.take(KT_ROWS * 1024)
    att = front.take(2, H_B, HD)
    att_sq = front.take(H_B, HD)
    zeros = front.take(W_B)
    top, ntop, den, rden = (front.take(2) for _ in range(4))
    ss, ln, rs = (front.take(H_B) for _ in range(3))
    s_bias = front.take(ROWS)
    s_new = front.take(2 * NS - DS)
    s_qbd = front.take(4, DB, NS)
    s_keys = Region(mem, END_W, MEM)
    kv1 = s_keys.take(KT_ROWS * 1024)
    s_probs = s_keys.take(ROWS + NS)
    s_probs_t = s_keys.take(KT_ROWS + 1, NS)
    s_kt = s_keys.take(4, NS)
    s_qkv = s_keys.take(3 * W_B)
    s_gain = s_keys.take(HD)
    s_out = s_keys.take(W_B)
    s_att = s_keys.take(2, HD)
    s_sq = s_keys.take(HD)
    s_sq2 = s_keys.take(HD)
    s_top, s_ntop, s_den, s_rden, s_ss, s_ln, s_rs = (s_keys.take(2) for _ in range(7))
    kv = [(t[:, 0:4 * ROWS].rearrange("p (j r) -> p j r", j=4), t[:, 4 * ROWS:].rearrange("p (t n) -> p t n", t=KT_ROWS)) for t in (kv0, kv1)]
    raw = kv0[:, 0:H_B * SEQ].rearrange("p (h x) -> p h x", h=H_B)
    s_raw = kv0[0:NS, H_B * SEQ:H_B * SEQ + ROWS + DS]
    flips = [(const["flip"], raw[:, n // 2, n % 2 * 512:(n % 2 + 1) * 512], bias[:, n // 2, n % 2 * 512:(n % 2 + 1) * 512]) for n in range(2 * H_B)]
    flips += [(const["flip8"][0:NS], s_raw[:, a:min(a + 512, ROWS)], s_bias[0:NS, a:min(a + 512, ROWS)]) for a in range(0, ROWS, 512)]
    flips += [(const["flip8"][0:NS], s_raw[:, ROWS:], s_new[0:NS, NS - DS:NS])]
    assert len(flips) == N_FLIPS
    steps = [(i, hh) for i in range(NT) for hh in range(H_B)]
    rows_of = scratch["qkv"].ap()

    def load_cache(eng, b):
        eng.dma_start(kv[b % 2][0], ins["keys_t"][b]).then_inc(sig[f"kv_in{b % 2}"], 16)
        eng.dma_start(kv[b % 2][1], ins["vals"][b]).then_inc(sig[f"kv_in{b % 2}"], 16)

    @block.sync
    def _(sp):
        sp.dma_start(qkv, rows_of[0:SEQ].rearrange("(t p) n -> p t n", p=P)).then_inc(sig["qkv_in"], 16)
        for hh in range(H_B):
            sp.dma_start(raw[:, hh], bass.AP(scratch["bias"], hh * LTAB + DMAX - SEQ + 1, [[1, P], [1, SEQ]])).then_inc(sig["raw_in"], 16)
        for hh in range(H_B):
            at = hh * LTAB
            part = slice(hh * DS, (hh + 1) * DS)
            sp.dma_start(s_raw[part, 0:ROWS_OLD].rearrange("p (g r) -> p g r", r=DS),
                         bass.AP(scratch["bias"], at, [[1, DS], [16, ROWS_OLD // DS], [1, DS]])).then_inc(sig["s_raw_in"], 16)
            sp.dma_start(s_raw[part, ROWS_OLD:ROWS], bass.AP(scratch["bias"], at + OLD, [[1, DS], [1, 512]])).then_inc(sig["s_raw_in"], 16)
            sp.dma_start(s_raw[part, ROWS:], bass.AP(scratch["bias"], at + WBUF, [[1, DS], [1, DS]])).then_inc(sig["s_raw_in"], 16)
        sp.wait_ge(sig["flipped"], N_FLIPS)
        load_cache(sp, 0)
        for i in range(NT):
            sp.wait_ge(sig["att"], i + 1)
            sp.dma_start(scratch["mix"].ap()[i * P:(i + 1) * P, W_A:], att[:, i % 2].rearrange("p h e -> p (h e)")).then_inc(sig[f"att_out{i % 2}"], 16)
        sp.wait_ge(sig["o_ps"], len(steps))
        sp.dma_start(s_qkv[0:NS], rows_of[SEQ:NTOK]).then_inc(sig["s_in"], 16)
        sp.dma_start(s_gain[0:NS], bc(ins["att_gain"].rearrange("a (h e) -> (a h) e", h=H_B), 1, DS)).then_inc(sig["s_in"], 16)
        load_cache(sp, 1)
        for b in range(DB):
            sp.wait_ge(sig["s_att"], b + 1)
            sp.dma_start(bass.AP(scratch["mix"], (SEQ + b * DS) * D + W_A, [[HD, H_B], [D, DS], [1, HD]]), s_att[0:NS, b % 2]).then_inc(sig[f"s_out{b % 2}"], 16)
            if b + 2 < DB:
                load_cache(sp, b + 2)
        for k in range(2):
            sp.wait_ge(sig[f"att_out{k}"], 16 * NT // 2)
            sp.wait_ge(sig[f"s_out{k}"], 16 * DB // 2)

    @block.gpsimd
    def _(pool):
        nc.gpsimd.memset(s_new, NEG).then_inc(sig["s_new_fill"], 1)
        nc.gpsimd.memset(s_qbd, 0.0).then_inc(sig["s_qbd_fill"], 1)
        nc.gpsimd.memset(zeros, 0.0).then_inc(sig["zeros"], 1)
        pool.wait_ge(sig["zeros"], 1)
        for n, name in enumerate(("k", "v")):
            new = rows_of[:, (n + 1) * W_B:(n + 2) * W_B]
            pool.dma_start(outs[name + "_p"][0:WBUF - SEQ].rearrange("(p r) n -> p r n", p=P), bc(zeros, 1, (WBUF - SEQ) // P)).then_inc(sig["window_out"], 16)
            pool.dma_start(outs[name + "_p"][WBUF - SEQ:WBUF], new[0:SEQ]).then_inc(sig["window_out"], 16)
            pool.dma_start(outs[name + "_s"][:, WBUF - DS:WBUF], new[SEQ:NTOK].rearrange("(b s) n -> b s n", b=DB)).then_inc(sig["window_out"], 16)
        pool.wait_ge(sig["window_out"], 16 * 6)
        pool.wait_ge(sig["cache_out"], 16 * 2 * DB)

    @block.tensor
    def _(pe):
        ident = const["ident"]
        pe.wait_ge(sig["raw_in"], 16 * H_B)
        pe.wait_ge(sig["s_raw_in"], 16 * 3 * H_B)
        for n, (selector, src, dst) in enumerate(flips):
            if n >= 8:
                pe.wait_ge(sig["flipped"], n - 7)
            nc.tensor.matmul(psum[0:dst.shape[0], n % 8, 0:dst.shape[1]], selector, src, start=True, stop=True).then_inc(sig["flip_ps"], 1)
        pe.wait_ge(sig["flipped"], N_FLIPS)
        pe.wait_ge(sig["qkv_in"], 16)
        for t in range(NT):
            for n in range(2):
                if t >= 4:
                    pe.wait_ge(sig["qk_t"], 2 * (t - 4) + n + 1)
                for j in range(4):
                    tr = nc.tensor.transpose(psum[:, 2 * (t % 4) + n, j * P:(j + 1) * P], qkv[:, t, n * W_B + j * P:n * W_B + (j + 1) * P], ident)
                tr.then_inc(sig["qk_t_ps"], 1)
        pe.wait_ge(sig["qk_t"], 2 * NT)

        def scores(n):
            i, hh = steps[n]
            if n >= 2:
                pe.wait_ge(sig["biased"], n - 1)
            half = slice(64 * (hh % 2), 64 * (hh % 2) + 64)
            for a in range(0, (i + 1) * P, 512):
                w = min(512, (i + 1) * P - a)
                mm = nc.tensor.matmul(psum[:, 2 * (n % 2) + a // 512, 0:w], q_t[half, hh // 2, i * P:(i + 1) * P], k_t[half, hh // 2, a:a + w], start=True, stop=True)
            mm.then_inc(sig["s2_ps"], 1)

        def turn(n):
            i, hh = steps[n]
            pe.wait_ge(sig["probs"], n + 1)
            if n >= 1:
                pe.wait_ge(sig["probs_t"], n)
            for t in range(i + 1):
                tr = nc.tensor.transpose(psum[:, 4 + t // 4, t % 4 * P:(t % 4 + 1) * P], probs[:, n % 2, t * P:(t + 1) * P], ident)
            tr.then_inc(sig["pt_ps"], 1)

        def values(n):
            i, hh = steps[n]
            pe.wait_ge(sig["probs_t"], n + 1)
            if n >= 2:
                pe.wait_ge(sig["o"], n - 1)
            cols = slice(2 * W_B + hh // 2 * P, 2 * W_B + (hh // 2 + 1) * P)
            for t in range(i + 1):
                mm = nc.tensor.matmul(psum[:, 6 + n % 2, 0:P], probs_t[:, n % 2, t], qkv[:, t, cols], start=t == 0, stop=t == i)
            mm.then_inc(sig["o_ps"], 1)

        for n in range(len(steps) + 2):
            if n < len(steps):
                scores(n)
            if 1 <= n <= len(steps):
                turn(n - 1)
            if n >= 2:
                values(n - 2)

        pe.wait_ge(sig["s_in"], 32)
        pe.wait_ge(sig["o"], len(steps))
        for n in range(2):
            for j in range(4):
                tr = nc.tensor.transpose(psum[:, 6 + n, j * NS:(j + 1) * NS], s_qkv[0:NS, n * W_B + j * P:n * W_B + (j + 1) * P], ident[0:NS, 0:NS])
        tr.then_inc(sig["s_t_ps"], 1)
        pe.wait_ge(sig["s_qbd"], 8)
        pe.wait_ge(sig["s_kt"], 1)

        def s_scores(b):
            keys, _ = kv[b % 2]
            pe.wait_ge(sig[f"kv_in{b % 2}"], 32 * (b // 2 + 1))
            if b >= 1:
                pe.wait_ge(sig["s_biased"], b)
            for a in range(0, ROWS, 512):
                w = min(512, ROWS - a)
                for j in range(4):
                    nc.tensor.matmul(psum[0:NS, a // 512, 0:w], s_qbd[:, j, b], keys[:, j, a:a + w], start=j == 0, stop=j == 3)
            for j in range(4):
                mm = nc.tensor.matmul(psum[0:NS, 2, 256:256 + NS], s_qbd[:, j, b], s_kt[:, j], start=j == 0, stop=j == 3)
            mm.then_inc(sig["s_s_ps"], 1)

        def s_values(b):
            _, vals = kv[b % 2]
            pe.wait_ge(sig["s_probs"], b + 1)
            for t in range(KT_ROWS + 1):
                m = P if t < KT_ROWS else NS
                tr = nc.tensor.transpose(psum[0:m, 4 + t // 8, t % 8 * NS:(t % 8 + 1) * NS], s_probs[0:NS, t * P:t * P + m], ident[0:NS, 0:NS])
            tr.then_inc(sig["s_pt_ps"], 1)
            pe.wait_ge(sig["s_probs_t"], b + 1)
            if b >= 1:
                pe.wait_ge(sig["s_o"], b)
            for t in range(KT_ROWS + 1):
                m = P if t < KT_ROWS else NS
                rhs = vals[:, t] if t < KT_ROWS else s_qkv[0:NS, 2 * W_B:]
                mm = nc.tensor.matmul(psum[0:NS, 3], s_probs_t[0:m, t], rhs, start=t == 0, stop=t == KT_ROWS)
            mm.then_inc(sig["s_o_ps"], 1)

        s_scores(0)
        for b in range(DB):
            if b + 1 < DB:
                s_scores(b + 1)
            s_values(b)

    @block.scalar
    def _(act):
        chain = Chain(act, sig["act2"])
        eps = const["eps"]
        for t in range(NT):
            for n in range(2):
                act.wait_ge(sig["qk_t_ps"], 2 * t + n + 1)
                dst = (q_t, k_t)[n][:, :, t * P:(t + 1) * P]
                nc.scalar.activation(dst, psum[:, 2 * (t % 4) + n].rearrange("p (j t) -> p j t", j=4), ACT.Copy, scale=(HD ** -0.5, 1.0)[n]).then_inc(sig["qk_t"], 1)

        def exps(n):
            i, hh = steps[n]
            act.wait_ge(sig["top"], n + 1)
            if n >= 2:
                act.wait_ge(sig["o"], n - 1)
            pr = probs[:, n % 2, 0:(i + 1) * P]
            nc.scalar.activation(pr, pr, ACT.Exp, bias=ntop[:, n % 2:n % 2 + 1], accum_out=den[:, n % 2:n % 2 + 1]).then_inc(sig["probs"], 1)

        def copy_t(n):
            i, hh = steps[n]
            act.wait_ge(sig["pt_ps"], n + 1)
            if n >= 2:
                act.wait_ge(sig["o_ps"], n - 1)
            nc.scalar.activation(probs_t[:, n % 2, 0:i + 1].rearrange("p t q -> p (t q)"), psum[:, 4:6].rearrange("p a n -> p (a n)")[:, 0:(i + 1) * P], ACT.Copy).then_inc(sig["probs_t"], 1)

        def head_rms(i):
            act.wait_ge(sig["ss"], i + 1)
            chain.link(nc.scalar.activation(ln, ss, ACT.Ln, scale=1.0 / HD, bias=eps))
            nc.scalar.activation(rs, ln, ACT.Exp, scale=-0.5).then_inc(sig["rs"], 1)

        for n in range(len(steps) + 3):
            if n < len(steps):
                exps(n)
            if 1 <= n <= len(steps):
                copy_t(n - 1)
            if n >= 10 and (n - 10) % 8 == 0:
                head_rms((n - 10) // 8)
        act.wait_ge(sig["s_t_ps"], 1)
        act.wait_ge(sig["s_qbd_fill"], 1)
        for j in range(4):
            for e in range(2):
                part = slice(64 * e, 64 * e + 64)
                col = (2 * j + e) * DS
                nc.scalar.activation(s_qbd[part, j, :, col:col + DS], psum[part, 6, j * NS:(j + 1) * NS].rearrange("p (b s) -> p b s", b=DB),
                                     ACT.Copy, scale=HD ** -0.5).then_inc(sig["s_qbd"], 1)
        nc.scalar.activation(s_kt, psum[:, 7, 0:4 * NS].rearrange("p (j t) -> p j t", j=4), ACT.Copy).then_inc(sig["s_kt"], 1)
        for b in range(DB):
            act.wait_ge(sig["s_top"], b + 1)
            pr = s_probs[0:NS]
            nc.scalar.activation(pr, pr, ACT.Exp, bias=s_ntop[0:NS, 0:1], accum_out=s_den[0:NS, 0:1]).then_inc(sig["s_probs"], 1)
            act.wait_ge(sig["s_pt_ps"], b + 1)
            if b >= 1:
                act.wait_ge(sig["s_o_ps"], b)
            flat = s_probs_t.rearrange("p t q -> p (t q)")
            chain.step(nc.scalar.activation(flat[:, 0:KT_ROWS * NS], psum[:, 4:6].rearrange("p a n -> p (a n)")[:, 0:KT_ROWS * NS], ACT.Copy))
            nc.scalar.activation(flat[0:NS, KT_ROWS * NS:], psum[0:NS, 5, (KT_ROWS - 8) * NS:(KT_ROWS - 7) * NS], ACT.Copy).then_inc(sig["s_probs_t"], 1)
            act.wait_ge(sig["s_raw"], b + 1)
            chain.link(nc.scalar.activation(s_sq[0:NS], s_att[0:NS, b % 2], ACT.Square, accum_out=s_ss[0:NS, 0:1]))
            chain.link(nc.scalar.activation(s_ln[0:NS, 0:1], s_ss[0:NS, 0:1], ACT.Ln, scale=1.0 / HD, bias=eps[0:NS]))
            nc.scalar.activation(s_rs[0:NS, 0:1], s_ln[0:NS, 0:1], ACT.Exp, scale=-0.5).then_inc(sig["s_rs"], 1)

    @block.vector
    def _(dve):
        v = nc.vector
        chain = Chain(dve, sig["dve2"])
        dve.wait_ge(sig["s_new_fill"], 1)
        for n, (_, _, dst) in enumerate(flips):
            dve.wait_ge(sig["flip_ps"], n + 1)
            v.tensor_copy(dst, psum[0:dst.shape[0], n % 8, 0:dst.shape[1]]).then_inc(sig["flipped"], 1)
        dve.wait_ge(sig["flipped"], N_FLIPS)

        def biased(n):
            i, hh = steps[n]
            w = (i + 1) * P
            dve.wait_ge(sig["s2_ps"], n + 1)
            if n >= 2:
                dve.wait_ge(sig["pt_ps"], n - 1)
            v.tensor_tensor_reduce(probs[:, n % 2, 0:w], psum[:, 2 * (n % 2):2 * (n % 2) + 2].rearrange("p a n -> p (a n)")[:, 0:w],
                                   bias[:, hh, SEQ - w:SEQ], 1.0, NEG, ALU.add, ALU.max, top[:, n % 2:n % 2 + 1]).then_inc(sig["biased"], 1)
            dve.wait_ge(sig["biased"], n + 1)
            v.tensor_scalar(ntop[:, n % 2:n % 2 + 1], top[:, n % 2:n % 2 + 1], -1.0, None, ALU.mult).then_inc(sig["top"], 1)

        def outputs(n):
            i, hh = steps[n]
            dve.wait_ge(sig["o_ps"], n + 1)
            chain.link(v.reciprocal(rden[:, n % 2:n % 2 + 1], den[:, n % 2:n % 2 + 1]))
            if hh == 0 and i >= 2:
                dve.wait_ge(sig[f"att_out{i % 2}"], 16 * (i // 2))
            v.tensor_scalar(att[:, i % 2, hh], psum[:, 6 + n % 2, 64 * (hh % 2):64 * (hh % 2) + 64], rden[:, n % 2:n % 2 + 1], None, ALU.mult).then_inc(sig["o"], 1)
            if hh == H_B - 1:
                dve.wait_ge(sig["o"], n + 1)
                chain.link(v.tensor_tensor(att_sq, att[:, i % 2], att[:, i % 2], ALU.mult))
                v.tensor_reduce(ss, att_sq, AX.X, ALU.add).then_inc(sig["ss"], 1)

        def normed(i):
            dve.wait_ge(sig["rs"], i + 1)
            chain.link(v.tensor_tensor(att[:, i % 2], att[:, i % 2], bc(rs, 2, HD), ALU.mult))
            v.tensor_tensor(att[:, i % 2], att[:, i % 2], const["att_gain"].rearrange("p (h e) -> p h e", h=H_B), ALU.mult).then_inc(sig["att"], 1)

        for n in range(len(steps) + 3):
            if n < len(steps):
                biased(n)
            if 2 <= n <= len(steps) + 1:
                outputs(n - 2)
            if n >= 10 and (n - 10) % 8 == 0:
                normed((n - 10) // 8)
        N = slice(0, NS)
        for b in range(DB):
            dve.wait_ge(sig["s_s_ps"], b + 1)
            if b == 0:
                dve.wait_ge(sig["s_in"], 32)
            else:
                dve.wait_ge(sig["s_pt_ps"], b)
            cells = psum[N, 0:3].rearrange("p a n -> p (a n)")
            chain.step(v.tensor_tensor_reduce(s_probs[N, 0:ROWS], cells[:, 0:ROWS], s_bias[N], 1.0, NEG, ALU.add, ALU.max, s_top[N, 0:1]))
            own = NS - DS - b * DS
            v.tensor_tensor_reduce(s_probs[N, ROWS:], cells[:, ROWS:ROWS + NS], s_new[N, own:own + NS], 1.0, NEG, ALU.add, ALU.max, s_top[N, 1:2]).then_inc(sig["s_biased"], 1)
            dve.wait_ge(sig["s_biased"], b + 1)
            chain.wait()
            chain.link(v.tensor_tensor(s_ntop[N, 1:2], s_top[N, 0:1], s_top[N, 1:2], ALU.max))
            v.tensor_scalar(s_ntop[N, 0:1], s_ntop[N, 1:2], -1.0, None, ALU.mult).then_inc(sig["s_top"], 1)
            dve.wait_ge(sig["s_probs"], b + 1)
            chain.link(v.reciprocal(s_rden[N, 0:1], s_den[N, 0:1]))
            dve.wait_ge(sig["s_o_ps"], b + 1)
            v.tensor_tensor(s_out[N].rearrange("p (h e) -> p h e", h=H_B), psum[N, 3].rearrange("p (h e) -> p h e", h=H_B), bc(const["headmask"][N], 2, HD), ALU.mult).then_inc(sig["s_o"], 1)
            dve.wait_ge(sig["s_o"], b + 1)
            chain.link(v.tensor_reduce(s_sq2[N], s_out[N].rearrange("p (h e) -> p e h", h=H_B), AX.X, ALU.add))
            if b >= 2:
                dve.wait_ge(sig[f"s_out{b % 2}"], 16 * (b // 2))
            v.tensor_scalar(s_att[N, b % 2], s_sq2[N], s_rden[N, 0:1], None, ALU.mult).then_inc(sig["s_raw"], 1)
            dve.wait_ge(sig["s_rs"], b + 1)
            v.scalar_tensor_tensor(out=s_att[N, b % 2], in0=s_att[N, b % 2], scalar=s_rs[N, 0:1], in1=s_gain[N], op0=ALU.mult, op1=ALU.mult).then_inc(sig["s_att"], 1)


C_TURN, C_TURNED, C_OUT, C_X1, C_SQ, C_H2, C_TURN2 = 1, 3, 6, 11, 18, 21, 26
C_Q = 30
C_PLACE = 98
C_EARLY = 118
HALF = PICKS // 2
N_SLOTS = 6


def stage3(nc, block, sig, mem, psum, const, ins, outs, scratch):
    work = Region(mem, N_CONST, MEM)
    w_out = work.take(KD, D)
    w_q = work.take(KD, 2 * HEADS * NKEY)
    keys_t = work.take(2, NKEY)
    mix = work.take(D)
    x1 = work.take(D)
    mod_a = work.take(D)
    mod_b = work.take(D)
    turned = work.take(KD, P)
    h2_next, h2 = work.take(D), work.take(D)
    q_t = work.take(2, P)
    found = work.take(2, NKEY)
    rest = work.take(2, NKEY)
    top_v = work.take(HEADS, 2, TOPK)
    top_i = work.take(HEADS, 2, TOPK).bitcast(U32)
    top_f = work.take(HEADS, 2, TOPK)
    cand = work.take(2, TOPK, TOPK)
    cand_rest = work.take(TOPK * TOPK)
    best_v = work.take(HEADS, TOPK)
    best_i = work.take(HEADS, TOPK).bitcast(U32)
    pos = work.take(2, PICKS).bitcast(U32)
    pos_f = work.take(2, PICKS)
    hot = work.take(4 * TOPK, TOPK)
    row_f = work.take(2, PICKS)
    idx_next, idx = work.take(PICKS).bitcast(U32), work.take(PICKS).bitcast(U32)
    gate_next, gate = work.take(PICKS), work.take(PICKS)
    total, share = work.take(HEADS), work.take(HEADS)
    dots, act_v, weight = work.take(PICKS), work.take(PICKS), work.take(PICKS)
    diag = work.take(4, P)
    ss, ln, rs = work.take(1), work.take(1), work.take(1)
    ring = work.take(N_SLOTS, 2, D)
    uses = [len(range(s, PICKS, N_SLOTS)) for s in range(N_SLOTS)]
    last_use = [s + N_SLOTS * (uses[s] - 1) for s in range(N_SLOTS)]

    def rows_at(i):
        return slice(SEQ, NTOK) if isinstance(i, int) and i == NT else bass.ds(i * P, P)

    def mod_rows(part, kind):
        at = scratch["mod"].ap()[:, part * D:(part + 1) * D]
        return at[0:1].broadcast_to((P, D)) if kind == "p" else bc(at[1:NC9], 1, DS)

    def each(engine, tile):
        tile(None, 0, P)
        tile(0, 1, P)
        with engine.Fori(1, NT - 1) as i:
            tile(i, i + 1, P)
        tile(NT - 1, NT, NS)
        tile(NT, None, NS)

    def rows_of(i):
        return NS if isinstance(i, int) and i == NT else P

    @block.sync
    def _(sp):
        sp.dma_start(w_out, ins["w_out"]).then_inc(sig["w_out_in"], 16)
        sp.dma_start(keys_t, ins["keys"]).then_inc(sig["keys_in"], 16)
        sp.dma_start(w_q, ins["w_q"]).then_inc(sig["w_q_in"], 16)

        def tile(i, n, _):
            if n is not None:
                r = rows_of(n)
                kind = "p" if r == P else "s"
                if i is not None:
                    sp.wait_ge(sig["y_out"], 16 * (n - 1))
                    apart(sp, sig["sp_passed"])
                sp.dma_start(mix[0:r], scratch["mix"].ap()[rows_at(n), :]).then_inc(sig["mix_in"], 16)
                sp.dma_start(x1[0:r], ins["x"][rows_at(n), :]).then_inc(sig["x1_in"], 16)
                sp.dma_start(mod_a[0:r], mod_rows(2, kind)).then_inc(sig["gate1_in"], 16)
                sp.dma_start(mod_b[0:r], mod_rows(4, kind)).then_inc(sig["gain2_in"], 16)
                sp.wait_ge(sig["x1"], n + 1)
                sp.dma_start(mod_a[0:r], mod_rows(3, kind)).then_inc(sig["shift2_in"], 16)
                sp.dma_start(scratch["x1"].ap()[rows_at(n), :], x1[0:r]).then_inc(sig["x1_out"], 16)
                sp.wait_ge(sig["h2"], n + 1)
                apart(sp, sig["sp_passed"])
                sp.wait_ge(sig["x1_out"], 16 * (n + 1))
            if i is not None:
                r = rows_of(i)
                kind = "p" if r == P else "s"
                if n is None:
                    sp.wait_ge(sig["y"], i)
                sp.dma_start(mod_a[0:r], mod_rows(5, kind)).then_inc(sig["gate2_in"], 16)
                sp.dma_start(x1[0:r], scratch["x1"].ap()[rows_at(i), :]).then_inc(sig["x1_back"], 16)
                sp.wait_ge(sig["y"], i + 1)
                apart(sp, sig["sp_passed"])
                sp.dma_start(outs["y"][rows_at(i), :], mix[0:r]).then_inc(sig["y_out"], 16)

        each(sp, tile)
        sp.wait_ge(sig["y_out"], 16 * (NT + 1))

    @block.gpsimd
    def _(pool):
        def tile(i, n, _):
            if i is None:
                return
            r = rows_of(i)
            for c in range(PICKS):
                s = c % N_SLOTS
                before = c - N_SLOTS if c >= N_SLOTS else last_use[s] - PICKS
                if c == 0:
                    pool.wait_ge(sig["idx_early"], i + 1)
                if c == HALF:
                    pool.wait_ge(sig["idx_late"], i + 1)
                pool.wait_ge(sig["summed"], i * PICKS + PICKS + before + 1)
                apart(pool, sig["pool_passed"])
                pool.indirect_dma_start(out=ring[0:r, s].rearrange("p a n -> p (a n)"), out_offset=None, in_=ins["experts"][:, :],
                                        in_offset=bass.IndirectOffsetOnAxis(ap=idx[0:r, c:c + 1], axis=0)).then_inc(sig[f"slot{s}"], 16)

        each(pool, tile)

    @block.tensor
    def _(pe):
        ident = const["ident"]

        def search(n, r, c):
            if c in (C_TURN, C_TURN + 1):
                half = c - C_TURN
                if half == 0:
                    pe.wait_ge(sig["mix_in"], 16 * (n + 1))
                for k in range(4 * half, 4 * half + 4):
                    tr = nc.tensor.transpose(psum[:, (2, 5)[half], k % 4 * P:k % 4 * P + r], mix[0:r, k * P:(k + 1) * P], ident[0:r, 0:r])
                tr.then_inc(sig["turned_ps"], 1)
            if C_OUT <= c < C_OUT + 8:
                half, k0 = (c - C_OUT) // 4, (c - C_OUT) % 4 * 2
                if c == C_OUT:
                    pe.wait_ge(sig["turned"], 4 * n + 2)
                    pe.wait_ge(sig["w_out_in"], 16)
                for k in (k0, k0 + 1):
                    mm = nc.tensor.matmul(psum[0:r, 3 + half], turned[:, k, 0:r], w_out[:, k, half * 512:(half + 1) * 512], start=k == 0, stop=k == KD - 1)
                if k0 == 6:
                    mm.then_inc(sig["mixed_ps"], 1)
            if c in (C_TURN2, C_TURN2 + 1):
                half = c - C_TURN2
                if half == 0:
                    pe.wait_ge(sig["h2"], n + 1)
                for k in range(4 * half, 4 * half + 4):
                    tr = nc.tensor.transpose(psum[:, (2, 5)[half], k % 4 * P:k % 4 * P + r], h2_next[0:r, k * P:(k + 1) * P], ident[0:r, 0:r])
                tr.then_inc(sig["turned_ps"], 1)
            j, phase = divmod(c - C_Q, 4)
            if c >= C_Q and j < 2 * HEADS and phase in (0, 1):
                if j == 0 and phase == 0:
                    pe.wait_ge(sig["turned"], 4 * n + 4)
                    pe.wait_ge(sig["w_q_in"], 16)
                if j >= 1 and phase == 0:
                    pe.wait_ge(sig["q"], 2 * HEADS * n + j)
                for k in range(4 * phase, 4 * phase + 4):
                    mm = nc.tensor.matmul(psum[:, 5, j % 4 * P:j % 4 * P + r], w_q[:, k, j * NKEY:(j + 1) * NKEY], turned[:, k, 0:r], start=k == 0, stop=k == KD - 1)
                if phase == 1:
                    mm.then_inc(sig["q_ps"], 1)
            if c >= C_Q and j < 2 * HEADS and phase == 3:
                pe.wait_ge(sig["q"], 2 * HEADS * n + j + 1)
                if j == 0:
                    pe.wait_ge(sig["keys_in"], 16)
                pe.wait_ge(sig["found"], 2 * HEADS * n + j - 1 if j >= 1 or not isinstance(n, int) or n else 0)
                nc.tensor.matmul(psum[0:r, 6 + j % 2, 0:NKEY], q_t[:, j % 2, 0:r], keys_t[:, j % 2], start=True, stop=True).then_inc(sig["s_ps"], 1)

        def tile(i, n, nr):
            for c in range(PICKS):
                if i is not None:
                    r = rows_of(i)
                    if c == 0:
                        pe.wait_ge(sig["acc_read"], 2 * i)
                    pe.wait_ge(sig["diag"], i * PICKS + c + 1)
                    for half in range(2):
                        mm = nc.tensor.matmul(psum[0:r, half], diag[0:r, c % 4, 0:r], ring[0:r, c % N_SLOTS, 1, half * 512:(half + 1) * 512], start=c == 0, stop=c == PICKS - 1)
                    mm.then_inc(sig["summed"], 1)
                if n is not None:
                    search(n, nr, c)

        each(pe, tile)

    @block.scalar
    def _(act):
        a = nc.scalar
        ident, eps = const["ident"], const["eps"]

        def search(n, r, c, chain):
            for first, at in ((0, C_TURNED), (2, C_TURN2 + 2)):
                if c in (at, at + 1):
                    half = c - at
                    act.wait_ge(sig["turned_ps"], 4 * n + first + half + 1)
                    a.activation(turned[:, 4 * half:4 * half + 4, 0:r], psum[:, (2, 5)[half]].rearrange("p (k t) -> p k t", k=4)[:, :, 0:r], ACT.Copy).then_inc(sig["turned"], 1)
            if c == C_SQ:
                act.wait_ge(sig["x1"], n + 1)
                chain.link(a.activation(mix[0:r], x1[0:r], ACT.Square, accum_out=ss[0:r]))
                chain.link(a.activation(ln[0:r], ss[0:r], ACT.Ln, scale=1.0 / D, bias=eps[0:r]))
                a.activation(rs[0:r], ln[0:r], ACT.Exp, scale=-0.5).then_inc(sig["rms2"], 1)
            j, phase = divmod(c - C_Q, 4)
            if c >= C_Q and j < 2 * HEADS and phase == 2:
                act.wait_ge(sig["q_ps"], 2 * HEADS * n + j + 1)
                if j >= 2:
                    act.wait_ge(sig["s_ps"], 2 * HEADS * n + j - 1)
                a.activation(q_t[:, j % 2, 0:r], psum[:, 5, j % 4 * P:j % 4 * P + r], ACT.Copy).then_inc(sig["q"], 1)
            if c == C_PLACE + 2:
                act.wait_ge(sig["gate_arg"], n + 1)
                a.activation(gate_next[0:r], gate_next[0:r], ACT.Exp).then_inc(sig["gate_exp"], 1)

        def tile(i, n, nr):
            chain = Chain(act, sig["act3"], 0 if i is None else 2 + i * (2 * PICKS + 2))
            for c in range(PICKS):
                if i is not None:
                    r = rows_of(i)
                    act.wait_ge(sig["dots"], i * PICKS + c + 1)
                    chain.link(a.activation(act_v[0:r, c:c + 1], dots[0:r, c:c + 1], ACT.Gelu))
                    chain.link(a.activation(weight[0:r, c:c + 1], act_v[0:r, c:c + 1], ACT.Copy, scale=gate[0:r, c:c + 1]))
                    before = i * PICKS + PICKS + c - 3
                    act.wait_ge(sig["summed"], before)
                    a.activation(diag[0:r, c % 4, 0:r], ident[0:r, 0:r], ACT.Copy, scale=weight[0:r, c:c + 1]).then_inc(sig["diag"], 1)
                if n is not None:
                    search(n, nr, c, chain)
            if i is not None:
                act.wait_ge(sig["summed"], i * PICKS + 2 * PICKS)
                if n is None:
                    act.wait_ge(sig["y_out"], 16 * i)
                act.wait_ge(sig["rms2"], min(i + 2, NT + 1) if isinstance(i, int) else i + 2)
                for half in range(2):
                    a.activation(mix[0:r, half * 512:(half + 1) * 512], psum[0:r, half], ACT.Copy).then_inc(sig["acc_read"], 1)

        each(act, tile)

    @block.vector
    def _(dve):
        v = nc.vector

        def search(n, r, c, chain):
            R = slice(0, r)
            if C_X1 <= c < C_X1 + 6:
                half, phase = (0, c - C_X1) if c < C_X1 + 3 else (1, c - C_X1 - 4)
                cols = slice(half * 512, (half + 1) * 512)
                if phase == 0:
                    if half == 0:
                        dve.wait_ge(sig["gate1_in"], 16 * (n + 1))
                        dve.wait_ge(sig["x1_in"], 16 * (n + 1))
                    dve.wait_ge(sig["mixed_ps"], 2 * n + half + 1)
                    chain.step(v.tensor_tensor(mod_a[R, cols], psum[R, 3 + half], mod_a[R, cols], ALU.mult))
                if phase == 1:
                    chain.wait()
                    op = v.tensor_tensor(x1[R, cols], x1[R, cols], mod_a[R, cols], ALU.add)
                    if half == 1:
                        op.then_inc(sig["x1"], 1)
                    else:
                        chain.step(op)
            if c == C_H2:
                dve.wait_ge(sig["rms2"], n + 1)
                dve.wait_ge(sig["gain2_in"], 16 * (n + 1))
                chain.step(v.scalar_tensor_tensor(out=h2_next[R], in0=x1[R], scalar=rs[R], in1=mod_b[R], op0=ALU.mult, op1=ALU.mult))
            if c == C_H2 + 2:
                dve.wait_ge(sig["shift2_in"], 16 * (n + 1))
                chain.wait()
                v.tensor_tensor(h2_next[R], h2_next[R], mod_a[R], ALU.add).then_inc(sig["h2"], 1)
            j, phase = divmod(c - C_Q - 4, 4)
            if c >= C_Q + 4 and j < 2 * HEADS and phase == 0:
                hh, half = divmod(j, 2)
                dve.wait_ge(sig["s_ps"], 2 * HEADS * n + j + 1)
                v.tensor_copy(found[R, j % 2], psum[R, 6 + j % 2, 0:NKEY]).then_inc(sig["found"], 1)
                dve.wait_ge(sig["found"], 2 * HEADS * n + j + 1)
                best(top_v[R, hh, half], top_i[R, hh, half], found[R, j % 2], rest[R, j % 2], chain)
            if c >= C_Q + 4 and j < 2 * HEADS and phase >= 2 and j % 2 == 1:
                hh = j // 2
                cd = cand[R, hh % 2]
                if phase == 2:
                    chain.link(v.tensor_tensor(cd, bc(top_v[R, hh, 0], 2, TOPK), bc(top_v[R, hh, 1], 1, TOPK), ALU.add))
                best(best_v[R, hh], best_i[R, hh], cd.rearrange("p a b -> p (a b)"), cand_rest[R], chain, ((0,), (8,))[phase - 2])
            if c == C_PLACE:
                chain.wait()
                chain.step(v.tensor_copy(top_f[R], top_i[R]))
                places = best_i[R].rearrange("p h k -> p (h k)")
                chain.step(v.tensor_scalar(pos[R, 0], places, 4, None, ALU.logical_shift_right))
                chain.step(v.tensor_scalar(pos[R, 1], places, TOPK - 1, None, ALU.bitwise_and))
                v.tensor_tensor(gate_next[R].rearrange("p (h k) -> p h k", h=HEADS), best_v[R], bc(best_v[R, :, 0], 2, TOPK), ALU.subtract).then_inc(sig["gate_arg"], 1)
            if c == C_PLACE + 1:
                chain.wait()
                chain.step(v.tensor_copy(pos_f[R], pos[R]))
            step = c - C_PLACE - 2
            if 0 <= step < 12:
                part, phase = divmod(step, 3)
                side, group = part % 2, part // 2
                places = pos_f[R, side, group * 64:(group + 1) * 64]
                chain.wait()
                if phase == 0:
                    chain.step(v.tensor_tensor(hot[R], bc(places, 2, TOPK), bc(const["iota16"][R], 1, 64), ALU.is_equal))
                if phase == 1:
                    hot4 = hot[R].rearrange("p (h k) a -> p h k a", h=4)
                    chain.step(v.tensor_tensor(hot4, hot4, bc(top_f[R, 4 * group:4 * group + 4, side], 2, TOPK), ALU.mult))
                if phase == 2:
                    chain.step(v.tensor_reduce(row_f[R, side, group * 64:(group + 1) * 64], hot[R], AX.X, ALU.add))
            if c == C_PLACE + 14:
                chain.wait()
                v.scalar_tensor_tensor(out=idx_next[R], in0=row_f[R, 0], scalar=float(NKEY), in1=row_f[R, 1], op0=ALU.mult, op1=ALU.add).then_inc(sig["idx_next"], 1)
                dve.wait_ge(sig["gate_exp"], n + 1)
                g3 = gate_next[R].rearrange("p (h k) -> p h k", h=HEADS)
                chain.link(v.tensor_reduce(total[R], g3, AX.X, ALU.add))
                chain.link(v.reciprocal(share[R], total[R]))
                chain.step(v.tensor_tensor(g3, g3, bc(share[R], 2, TOPK), ALU.mult))

        def best(values, places, src, left, chain, eights=(0, 8)):
            for at in eights:
                if at == 8:
                    src = left
                    chain.wait()
                apart(dve, sig["dve_passed"])
                chain.link(v.max(values[:, at:at + 8], src))
                apart(dve, sig["dve_passed"])
                chain.step(v.max_index(places[:, at:at + 8], values[:, at:at + 8], src))
                if at == 0:
                    chain.step(v.match_replace(left, values[:, 0:8], src, -3.0e38))

        def hand_over(n, r, part, chain):
            cols = slice(part * HALF, (part + 1) * HALF)
            chain.wait()
            if part == 0:
                dve.wait_ge(sig["idx_next"], n + 1)
            chain.step(v.tensor_copy(gate[0:r, cols], gate_next[0:r, cols]))
            chain.wait()
            v.tensor_copy(idx[0:r, cols], idx_next[0:r, cols]).then_inc(sig[("idx_early", "idx_late")[part]], 1)

        def tile(i, n, nr):
            base = 0 if i is None else PER_SEARCH + i * PER_TILE
            chain = Chain(dve, sig["dve3"], base)
            for c in range(PICKS):
                if i is not None:
                    r = rows_of(i)
                    s = c % N_SLOTS
                    dve.wait_ge(sig[f"slot{s}"], 16 * (i * uses[s] + c // N_SLOTS + 1))
                    row = ring[0:r, s, 0]
                    v.tensor_tensor_reduce(row, row, h2[0:r], 1.0, 0.0, ALU.mult, ALU.add, dots[0:r, c:c + 1]).then_inc(sig["dots"], 1)
                if n is not None:
                    search(n, nr, c, chain)
                    if c == C_EARLY:
                        hand_over(n, nr, 0, chain)
            if i is not None:
                dve.wait_ge(sig["dots"], i * PICKS + PICKS)
                dve.wait_ge(sig["diag"], i * PICKS + PICKS)
            if n is not None:
                hand_over(n, nr, 1, chain)
                chain.link(v.tensor_copy(h2[0:nr], h2_next[0:nr]))
            if i is not None:
                dve.wait_ge(sig["acc_read"], 2 * i + 2)
                dve.wait_ge(sig["gate2_in"], 16 * (i + 1))
                dve.wait_ge(sig["x1_back"], 16 * (i + 1))
                chain.link(v.tensor_tensor(mix[0:r], mix[0:r], mod_a[0:r], ALU.mult))
                v.tensor_tensor(mix[0:r], mix[0:r], x1[0:r], ALU.add).then_inc(sig["y"], 1)
            want = PER_SEARCH if i is None else PER_TILE
            assert chain.n == want or n is None, (chain.n, want)

        v.memset(dots, 0.0).then_inc(sig["summed"], PICKS)
        each(dve, tile)


INPUTS = ("x", "cond", "const", "onehot", "rel", "w_ada", "b_ada", "norm_gain", "w_in", "qk_gain", "b_gate", "mo_gain", "att_gain", "conv",
          "state", "m0", "conv_tail", "cache_k", "cache_v", "keys_t", "vals", "w_out", "w_q", "keys", "experts")


def lay_out(a):
    f = np.float32
    g = {k: np.asarray(v) for k, v in a.items()}

    def blocks(w):
        return np.ascontiguousarray(w.reshape(-1, P, w.shape[-1]).transpose(1, 0, 2))

    cond = np.concatenate([g["c_prompt"], g["c_sample"]])
    rel = np.zeros((P, H_B), f)
    rel[:N_BUCKETS] = g["rel_bias"]
    rel[N_BUCKETS] = 1.0
    state = np.concatenate([g["state_C"][0], g["state_n"][0][..., None]], -1)
    seen = np.concatenate([np.arange(OLD).reshape(-1, 16)[:, :DS].ravel(), np.arange(OLD, WBUF)])
    cache_k, cache_v = (g[n][0].reshape(DB, WBUF, W_B) for n in ("cache_k", "cache_v"))
    return {
        "w_out": blocks(g["w_out"][0]), "w_q": blocks(g["peer_wq"][0]),
        "keys": np.ascontiguousarray(g["peer_keys"][0].transpose(2, 0, 1)),
        "experts": np.concatenate([g["peer_u"][0], g["peer_v"][0]], 1),
        "cache_k": cache_k, "cache_v": cache_v,
        "keys_t": np.ascontiguousarray(cache_k[:, seen].transpose(0, 2, 1).reshape(DB, 4, P, ROWS).transpose(0, 2, 1, 3)),
        "vals": np.ascontiguousarray(cache_v[:, seen].reshape(DB, KT_ROWS, P, W_B).transpose(0, 2, 1, 3)),
        "x": np.concatenate([g["x_prompt"].reshape(SEQ, D), g["x_sample"].reshape(NS, D)]),
        "cond": blocks(cond.T),
        "const": CONST, "onehot": ONEHOT, "rel": rel,
        "w_ada": blocks(g["w_ada"][0]), "b_ada": g["b_ada"],
        "norm_gain": np.concatenate([g["norm1_g"], g["norm2_g"]]),
        "w_in": blocks(g["w_in"][0]),
        "qk_gain": np.concatenate([g["q_norm_g"], g["k_norm_g"]], 1),
        "b_gate": g["b_gate"],
        "mo_gain": g["mlstm_out_g"].reshape(1, W_A), "att_gain": g["att_out_g"].reshape(1, W_B),
        "conv": np.ascontiguousarray(np.concatenate([g["conv_w"][0], g["conv_b"]]).reshape(CONV_W + 1, 8, P).transpose(2, 0, 1)),
        "state": np.ascontiguousarray(state.transpose(2, 0, 1, 3)),
        "m0": np.repeat(g["state_m"][0], DS, 0),
        "conv_tail": np.ascontiguousarray(g["state_conv"][0].reshape(DB, HALO, 8, P).transpose(3, 2, 0, 1)),
    }


OUTS = {
    "state_p": (P, H_A, DK + 1), "m_p": (1, H_A), "conv_p": (P, 8, HALO),
    "state_s": (P, DB, H_A, DK + 1), "m_s": (NS, H_A), "conv_s": (P, 8, DB, HALO),
    "k_p": (WBUF, W_B), "v_p": (WBUF, W_B), "k_s": (DB, WBUF, W_B), "v_s": (DB, WBUF, W_B),
    "y": (NTOK, D),
}


def kernel(**inputs):
    import concourse.bacc as bacc
    from concourse.bass_utils import run_bass_kernel_spmd

    laid = lay_out(inputs)
    nc = bacc.Bacc("TRN2", target_bir_lowering=False, num_devices=1)
    ins = {n: nc.dram_tensor("in_" + n, laid[n].shape, mybir.dt.from_np(laid[n].dtype), kind="ExternalInput").ap() for n in INPUTS}
    outs = {n: nc.dram_tensor("out_" + n, s, F32, kind="ExternalOutput").ap() for n, s in OUTS.items()}
    layer(nc, ins, outs)
    got = run_bass_kernel_spmd(nc, [{"in_" + n: laid[n] for n in INPUTS}], core_ids=[0]).results[0]
    o = {n: np.asarray(got["out_" + n]) for n in OUTS}
    state_p, state_s = o["state_p"].transpose(1, 0, 2), o["state_s"].transpose(1, 2, 0, 3)
    m_s = o["m_s"].reshape(DB, DS, H_A)[:, 0]
    window = (WBUF, H_B, HD)
    return (
        o["y"][:SEQ].reshape(1, SEQ, D), o["y"][SEQ:].reshape(DB, DS, D),
        o["k_p"].reshape(1, 1, *window), o["v_p"].reshape(1, 1, *window),
        np.ascontiguousarray(o["conv_p"].transpose(2, 1, 0)).reshape(1, 1, HALO, 2 * W_A),
        np.ascontiguousarray(state_p[..., :DK])[None, None], np.ascontiguousarray(state_p[..., DK])[None, None], o["m_p"].reshape(1, 1, H_A),
        o["k_s"].reshape(1, DB, *window), o["v_s"].reshape(1, DB, *window),
        np.ascontiguousarray(o["conv_s"].transpose(2, 3, 1, 0)).reshape(1, DB, HALO, 2 * W_A),
        np.ascontiguousarray(state_s[..., :DK])[None], np.ascontiguousarray(state_s[..., DK])[None], np.ascontiguousarray(m_s)[None],
    )
```
